# Optimizing a Trainium2 kernel written in Bass

```python
import jax, jax.numpy as jnp
from jax import lax
import numpy as np

D_MODEL = 1024
BATCH = 1
SEQ = 1024
DEPTH = 2
DEC_BATCH = 8
DEC_SEQ = 4
PAST_LEN = 2048
PAGE_SIZE = 128

N_EVEN = (DEPTH + 1) // 2
N_ODD = DEPTH // 2
W_CONV = D_MODEL // 2
CONV_WIDTH = 31
N_HEADS = 8
HEAD_DIM = 64
KV_HEADS = 2
GROUP = N_HEADS // KV_HEADS
W_ATTN = N_HEADS * HEAD_DIM
KV_W = 2 * KV_HEADS * HEAD_DIM
CMP_STRIDE = 16
CMP_BLOCK = 2 * CMP_STRIDE
SEL_BLOCK = 64
N_SEL = 16
WINDOW = 512
Q_BLOCK = 128
W_POOL = D_MODEL
POOL_WINDOWS = (2, 4, 8, 16)
N_POOL_GROUPS = 4
POOL_GROUP_W = W_POOL // N_POOL_GROUPS
POOL_MAX = 16
LN_EPS = 1e-5
NEG_INF = -1e30
SEL_FORCE = 1e9
DEEPNORM_ALPHA = (2 * DEPTH) ** 0.25
DEEPNORM_BETA = (8 * DEPTH) ** -0.25
EVEN_SPLITS = (W_CONV, W_CONV, W_CONV, W_ATTN, KV_W, KV_W, KV_W, 3 * N_HEADS, W_ATTN)
E_IN = 3 * W_CONV + 2 * W_ATTN + 3 * KV_W + 3 * N_HEADS

kernel_name = 'hybrid_conv_nsa_pool_decoder_step'

def layer_norm(x, g, b):
    xf = x.astype(jnp.float32)
    mu = xf.mean(-1, keepdims=True)
    var = jnp.square(xf - mu).mean(-1, keepdims=True)
    y = (xf - mu) * lax.rsqrt(var + LN_EPS) * g.astype(jnp.float32) + b.astype(jnp.float32)
    return y.astype(x.dtype)

def masked_softmax(s, mask):
    s = jnp.where(mask, s.astype(jnp.float32), NEG_INF)
    return jax.nn.softmax(s, axis=-1) * mask

def even_project(x, w_in):
    B, T, _ = x.shape
    h = jnp.einsum('btd,de->bte', x, w_in)
    offsets = np.cumsum(EVEN_SPLITS)[:-1].tolist()
    a_val, a_glu, a_gate, q, kv_c, kv_s, kv_w, g, b_gate = jnp.split(h, offsets, axis=-1)
    kv_shape = (B, T, 2, KV_HEADS, HEAD_DIM)
    u = a_val * jax.nn.sigmoid(a_glu)
    return (u, a_gate, q.reshape(B, T, N_HEADS, HEAD_DIM), kv_c.reshape(kv_shape),
            kv_s.reshape(kv_shape), kv_w.reshape(kv_shape), g.reshape(B, T, N_HEADS, 3), b_gate)

def conv_branch(u_ext, a_gate, conv_w, conv_b, ln_g, ln_b):
    y = lax.conv_general_dilated(u_ext, conv_w[:, None, :], (1,), 'VALID',
                                 dimension_numbers=('NWC', 'WIO', 'NWC'),
                                 feature_group_count=W_CONV) + conv_b
    return jax.nn.silu(layer_norm(y, ln_g, ln_b)) * jax.nn.silu(a_gate)

def compress_kv(kv, w_cmp):
    B, L = kv.shape[:2]
    n_ch = L // CMP_STRIDE
    ch = kv[:, :n_ch * CMP_STRIDE].reshape(B, n_ch, CMP_STRIDE, 2, KV_HEADS, HEAD_DIM)
    kc = (jnp.einsum('bnjchd,jchd->bnchd', ch[:, :-1], w_cmp[:CMP_STRIDE])
          + jnp.einsum('bnjchd,jchd->bnchd', ch[:, 1:], w_cmp[CMP_STRIDE:]))
    kc_end = jnp.arange(n_ch - 1) * CMP_STRIDE + (CMP_BLOCK - 1)
    return kc[:, :, 0], kc[:, :, 1], kc_end

def select_blocks(kv):
    B, L = kv.shape[:2]
    ns = -(-L // SEL_BLOCK)
    kv = jnp.pad(kv, ((0, 0), (0, ns * SEL_BLOCK - L), (0, 0), (0, 0), (0, 0)))
    kv = kv.reshape(B, ns, SEL_BLOCK, 2, KV_HEADS, HEAD_DIM).transpose(3, 0, 4, 1, 2, 5)
    return kv[0], kv[1]

def nsa_block(q, g, q_pos, kc, vc, kc_end, ks, vs, kw, vw, kw_pos):
    B, Q = q.shape[:2]
    qg = q.reshape(B, Q, KV_HEADS, GROUP, HEAD_DIM) * (HEAD_DIM ** -0.5)
    s_c = jnp.einsum('bqhgd,bnhd->bhgqn', qg, kc)
    p_c = masked_softmax(s_c, kc_end[None, :] <= q_pos[:, None])
    o_c = jnp.einsum('bhgqn,bnhd->bqhgd', p_c.astype(vc.dtype), vc)
    ns, nc = ks.shape[2], kc.shape[1]
    per = SEL_BLOCK // CMP_STRIDE
    p_grp = jnp.pad(p_c.sum(2), ((0, 0), (0, 0), (0, 0), (0, per * ns - nc)))
    score = p_grp.reshape(B, KV_HEADS, Q, ns, per)[..., :per - 1].sum(-1)
    blk = jnp.arange(ns)[None, :]
    cur = (q_pos // SEL_BLOCK)[:, None]
    forced = (blk == 0) | ((blk >= cur - 1) & (blk <= cur))
    score = jnp.where(forced, SEL_FORCE, jnp.where(blk <= cur, score, -SEL_FORCE))
    n_top = min(N_SEL, ns)
    _, idx = lax.top_k(score, n_top)
    bi = jnp.arange(B)[:, None, None, None]
    hi = jnp.arange(KV_HEADS)[None, :, None, None]
    n_keys = n_top * SEL_BLOCK
    k_sel = ks[bi, hi, idx].reshape(B, KV_HEADS, Q, n_keys, HEAD_DIM)
    v_sel = vs[bi, hi, idx].reshape(B, KV_HEADS, Q, n_keys, HEAD_DIM)
    pos_sel = (idx[..., None] * SEL_BLOCK + jnp.arange(SEL_BLOCK)).reshape(B, KV_HEADS, Q, n_keys)
    s_s = jnp.einsum('bqhgd,bhqnd->bhgqn', qg, k_sel)
    p_s = masked_softmax(s_s, (pos_sel <= q_pos[:, None])[:, :, None])
    o_s = jnp.einsum('bhgqn,bhqnd->bqhgd', p_s.astype(v_sel.dtype), v_sel)
    rel = q_pos[:, None] - kw_pos[None, :]
    s_w = jnp.einsum('bqhgd,bwhd->bhgqw', qg, kw)
    p_w = masked_softmax(s_w, (rel >= 0) & (rel < WINDOW) & (kw_pos[None, :] >= 0))
    o_w = jnp.einsum('bhgqw,bwhd->bqhgd', p_w.astype(vw.dtype), vw)
    gq = jax.nn.sigmoid(g.reshape(B, Q, KV_HEADS, GROUP, 3).astype(jnp.float32)).astype(q.dtype)
    o = gq[..., 0:1] * o_c + gq[..., 1:2] * o_s + gq[..., 2:3] * o_w
    return o.reshape(B, Q, W_ATTN)

def mixer_out(a_out, b_out, b_gate, w_out):
    h = jnp.concatenate([a_out, b_out * jax.nn.silu(b_gate)], axis=-1)
    return jnp.einsum('bte,ed->btd', h, w_out)

def even_prompt(x, w_in, w_cmp, conv_w, conv_b, ln_g, ln_b, w_out):
    B, T, _ = x.shape
    u, a_gate, q, kv_c, kv_s, kv_w, g, b_gate = even_project(x, w_in)
    u_ext = jnp.pad(u, ((0, 0), (CONV_WIDTH - 1, 0), (0, 0)))
    a_out = conv_branch(u_ext, a_gate, conv_w, conv_b, ln_g, ln_b)
    kc, vc, kc_end = compress_kv(kv_c, w_cmp)
    ks, vs = select_blocks(kv_s)
    kw_pad = jnp.pad(kv_w, ((0, 0), (WINDOW, 0), (0, 0), (0, 0), (0, 0)))
    n_qb = T // Q_BLOCK
    q_b = jnp.swapaxes(q.reshape(B, n_qb, Q_BLOCK, N_HEADS, HEAD_DIM), 0, 1)
    g_b = jnp.swapaxes(g.reshape(B, n_qb, Q_BLOCK, N_HEADS, 3), 0, 1)

    def query_block(args):
        i, q_i, g_i = args
        start = i * Q_BLOCK
        kw_i = lax.dynamic_slice_in_dim(kw_pad, start, WINDOW + Q_BLOCK, axis=1)
        q_pos = start + jnp.arange(Q_BLOCK)
        kw_pos = start - WINDOW + jnp.arange(WINDOW + Q_BLOCK)
        return nsa_block(q_i, g_i, q_pos, kc, vc, kc_end, ks, vs, kw_i[:, :, 0], kw_i[:, :, 1], kw_pos)

    b_out = lax.map(query_block, (jnp.arange(n_qb), q_b, g_b))
    b_out = jnp.swapaxes(b_out, 0, 1).reshape(B, T, W_ATTN)
    y = mixer_out(a_out, b_out, b_gate, w_out)
    return y, kv_c, kv_s, kv_w[:, -min(WINDOW, T):], u_ext[:, -(CONV_WIDTH - 1):]

def even_sample(x, cache_c, cache_s, win_buf, conv_buf, page_table, w_in, w_cmp, conv_w, conv_b, ln_g, ln_b, w_out):
    B, T, _ = x.shape
    past_len = page_table.shape[1] * cache_c.shape[1]
    u, a_gate, q, kv_c, kv_s, kv_w, g, b_gate = even_project(x, w_in)
    u_ext = jnp.concatenate([conv_buf.astype(u.dtype), u], axis=1)
    a_out = conv_branch(u_ext, a_gate, conv_w, conv_b, ln_g, ln_b)

    def paged_rows(cache, new):
        past = cache[page_table].reshape((B, past_len) + cache.shape[2:])
        return jnp.concatenate([past.astype(new.dtype), new], axis=1)

    kc, vc, kc_end = compress_kv(paged_rows(cache_c, kv_c), w_cmp)
    ks, vs = select_blocks(paged_rows(cache_s, kv_s))
    win_ext = jnp.concatenate([win_buf.astype(kv_w.dtype), kv_w], axis=1)
    w_len = win_ext.shape[1]
    q_pos = past_len + jnp.arange(T)
    kw_pos = past_len + T - w_len + jnp.arange(w_len)
    b_out = nsa_block(q, g, q_pos, kc, vc, kc_end, ks, vs, win_ext[:, :, 0], win_ext[:, :, 1], kw_pos)
    y = mixer_out(a_out, b_out, b_gate, w_out)
    return y, kv_c, kv_s, win_ext[:, -min(WINDOW, w_len):], u_ext[:, -(CONV_WIDTH - 1):]

def pool_mixer(x, buf, pos0, w_in, w_grp, scale, w_out):
    B, T, _ = x.shape
    v, gate = jnp.split(jnp.einsum('btd,de->bte', x, w_in), 2, axis=-1)
    P = POOL_MAX - 1
    ext = jnp.concatenate([buf.astype(v.dtype), v], axis=1)
    cs = jnp.pad(jnp.cumsum(ext.astype(jnp.float32), axis=1), ((0, 0), (1, 0), (0, 0)))
    pos = pos0 + jnp.arange(T)
    means = []
    for gi, w in enumerate(POOL_WINDOWS):
        c0, c1 = gi * POOL_GROUP_W, (gi + 1) * POOL_GROUP_W
        win_sum = cs[:, P + 1:P + 1 + T, c0:c1] - cs[:, P + 1 - w:P + 1 - w + T, c0:c1]
        cnt = jnp.minimum(pos + 1, w).astype(jnp.float32)[None, :, None]
        means.append(win_sum / cnt)
    mean = jnp.stack(means, axis=2)
    d = (mean - v.reshape(B, T, N_POOL_GROUPS, POOL_GROUP_W).astype(jnp.float32)).astype(v.dtype)
    mixed = jnp.einsum('btgc,gce->btge', d, w_grp).reshape(B, T, W_POOL) * scale
    y = jnp.einsum('bte,ed->btd', mixed * jax.nn.silu(gate), w_out)
    return y, ext[:, -P:]

def setup_inputs(seed: int = 0) -> dict:
    key = jax.random.key(seed)
    ks = jax.random.split(key, 24)
    n_pages = PAST_LEN // PAGE_SIZE
    n_phys = (DEC_BATCH * n_pages * 5) // 4
    win_buf = min(WINDOW, PAST_LEN)
    nrm = jax.random.normal
    f32 = jnp.float32
    page_table = jax.random.permutation(ks[0], n_phys)[:DEC_BATCH * n_pages].reshape(DEC_BATCH, n_pages).astype(jnp.int32)
    cache_shape = (N_EVEN, n_phys, PAGE_SIZE, 2, KV_HEADS, HEAD_DIM)
    return {
        'x_prompt': nrm(ks[1], (BATCH, SEQ, D_MODEL), f32),
        'x_sample': nrm(ks[2], (DEC_BATCH, DEC_SEQ, D_MODEL), f32),
        'cache_kv_cmp': nrm(ks[3], cache_shape, f32),
        'cache_kv_sel': nrm(ks[4], cache_shape, f32),
        'state_win_kv': nrm(ks[5], (N_EVEN, DEC_BATCH, win_buf, 2, KV_HEADS, HEAD_DIM), f32),
        'state_conv': 0.5 * nrm(ks[6], (N_EVEN, DEC_BATCH, CONV_WIDTH - 1, W_CONV), f32),
        'state_pool': nrm(ks[7], (N_ODD, DEC_BATCH, POOL_MAX - 1, W_POOL), f32),
        'page_table': page_table,
        'w_in_even': nrm(ks[8], (N_EVEN, D_MODEL, E_IN), f32) * D_MODEL ** -0.5,
        'w_cmp': (1.0 + 0.1 * nrm(ks[9], (N_EVEN, CMP_BLOCK, 2, KV_HEADS, HEAD_DIM), f32)) / CMP_BLOCK,
        'conv_w': nrm(ks[10], (N_EVEN, CONV_WIDTH, W_CONV), f32) * CONV_WIDTH ** -0.5,
        'conv_b': 0.02 * nrm(ks[11], (N_EVEN, W_CONV), f32),
        'conv_ln_g': 1.0 + 0.05 * nrm(ks[12], (N_EVEN, W_CONV), f32),
        'conv_ln_b': 0.02 * nrm(ks[13], (N_EVEN, W_CONV), f32),
        'w_out_even': nrm(ks[14], (N_EVEN, W_CONV + W_ATTN, D_MODEL), f32) * (W_CONV + W_ATTN) ** -0.5 * DEEPNORM_BETA,
        'w_in_odd': nrm(ks[15], (N_ODD, D_MODEL, 2 * W_POOL), f32) * D_MODEL ** -0.5,
        'w_pool_grp': nrm(ks[16], (N_ODD, N_POOL_GROUPS, POOL_GROUP_W, POOL_GROUP_W), f32) * POOL_GROUP_W ** -0.5,
        'pool_scale': 1.0 + 0.05 * nrm(ks[17], (N_ODD, W_POOL), f32),
        'w_out_odd': nrm(ks[18], (N_ODD, W_POOL, D_MODEL), f32) * W_POOL ** -0.5 * DEEPNORM_BETA,
        'ln_g': 1.0 + 0.05 * nrm(ks[19], (DEPTH, D_MODEL), f32),
        'ln_b': 0.02 * nrm(ks[20], (DEPTH, D_MODEL), f32),
    }

def reference(x_prompt, x_sample, cache_kv_cmp, cache_kv_sel, state_win_kv, state_conv, state_pool, page_table,
              w_in_even, w_cmp, conv_w, conv_b, conv_ln_g, conv_ln_b, w_out_even,
              w_in_odd, w_pool_grp, pool_scale, w_out_odd, ln_g, ln_b):
    xp, xs = x_prompt, x_sample
    past_len = page_table.shape[1] * cache_kv_cmp.shape[2]
    kvc_p, kvs_p, win_p, conv_p, pool_p = [], [], [], [], []
    kvc_s, kvs_s, win_s, conv_s, pool_s = [], [], [], [], []
    for layer in range(DEPTH):
        j = layer // 2
        if layer % 2 == 0:
            dp, a1, a2, a3, a4 = even_prompt(xp, w_in_even[j], w_cmp[j], conv_w[j], conv_b[j],
                                             conv_ln_g[j], conv_ln_b[j], w_out_even[j])
            ds, b1, b2, b3, b4 = even_sample(xs, cache_kv_cmp[j], cache_kv_sel[j], state_win_kv[j], state_conv[j],
                                             page_table, w_in_even[j], w_cmp[j], conv_w[j], conv_b[j],
                                             conv_ln_g[j], conv_ln_b[j], w_out_even[j])
            kvc_p.append(a1); kvs_p.append(a2); win_p.append(a3); conv_p.append(a4)
            kvc_s.append(b1); kvs_s.append(b2); win_s.append(b3); conv_s.append(b4)
        else:
            buf0 = jnp.zeros((xp.shape[0], POOL_MAX - 1, W_POOL), xp.dtype)
            dp, a5 = pool_mixer(xp, buf0, 0, w_in_odd[j], w_pool_grp[j], pool_scale[j], w_out_odd[j])
            ds, b5 = pool_mixer(xs, state_pool[j], past_len, w_in_odd[j], w_pool_grp[j], pool_scale[j], w_out_odd[j])
            pool_p.append(a5); pool_s.append(b5)
        xp = layer_norm(DEEPNORM_ALPHA * xp + dp, ln_g[layer], ln_b[layer])
        xs = layer_norm(DEEPNORM_ALPHA * xs + ds, ln_g[layer], ln_b[layer])
    return (xp, xs,
            jnp.stack(kvc_p), jnp.stack(kvs_p), jnp.stack(win_p), jnp.stack(conv_p), jnp.stack(pool_p),
            jnp.stack(kvc_s), jnp.stack(kvs_s), jnp.stack(win_s), jnp.stack(conv_s), jnp.stack(pool_s))


_drawn_inputs = setup_inputs


def setup_inputs(seed=0):
    import zlib

    import numpy as np

    out = dict(_drawn_inputs(seed))
    spreads = {}
    factors = {'cache_kv_cmp': 8.0,
     'cache_kv_sel': 8.0,
     'w_cmp': 8.0,
     'conv_b': 8.0,
     'conv_ln_g': 8.0,
     'conv_ln_b': 27.746,
     'pool_scale': 6.212}
    for name, (base, spread) in spreads.items():
        noise = np.random.default_rng([zlib.crc32(name.encode()), seed]).standard_normal(out[name].shape)
        drawn = base * np.exp(spread * noise) if base else spread * noise
        out[name] = __import__('jax').numpy.asarray(drawn.astype(out[name].dtype))
    for name, factor in factors.items():
        out[name] = (out[name] * factor).astype(out[name].dtype)
    return out
```

```python
from contextlib import ExitStack

import numpy as np
import concourse.bass as bass
from concourse import mybir

F32 = mybir.dt.float32
F32R = mybir.dt.float32r
BF16 = mybir.dt.bfloat16
I32 = mybir.dt.int32
ALU = mybir.AluOpType
ACT = mybir.ActivationFunctionType
AX = mybir.AxisListType.X

P = 128
D = 1024
SEQ = 1024
DB, DS = 8, 4
NSAMP = DB * DS
T = SEQ + NSAMP
CH = T // 3
KT = D // P
NTT = SEQ // P + 1
WC = 512
CW = 31
HD = 64
GROUP = 4
PAST, PAGE = 2048, 128
NPG = PAST // PAGE
CSTR = 16
NCP = SEQ // CSTR - 1
NCS = (PAST + DS) // CSTR - 1
SELB = 64
NBLK = PAST // SELB
NFREE = NBLK - 2
NPICK = 16 - 3
WIN = 512
PMAX = 16
ALPHA = 4.0 ** 0.25
EPS = 1e-5
NEG = -1e30
SCALE = HD ** -0.5
O_VAL, O_GLU, O_AG, O_Q, O_KV, O_G, O_BG = 0, 512, 1024, 1536, 2048, 2816, 2840
E_IN = 3352
UW = CW - 1 + SEQ
US = CW - 1 + DS
VW = PMAX - 1 + SEQ
VS = PMAX - 1 + DS

NM = 26
M_KV, M_Q, M_BG, M_AG = 8, 14, 18, 22


def tok(tt):
    return slice(tt * P, min(tt * P + P, T))


def ntok(tt):
    return min(P, T - tt * P)


def program(nc, x_prompt, x_sample, cache_kv_cmp, cache_kv_sel, state_win_kv, state_conv, state_pool, page_table,
            w_in_even, w_cmp, conv_w, conv_b, conv_ln_g, conv_ln_b, w_out_even, w_in_odd, w_pool_grp, pool_scale,
            w_out_odd, ln_g, ln_b, y_prompt, y_sample, o_kvc_p, o_kvs_p, o_win_p, o_conv_p, o_pool_p,
            o_kvc_s, o_kvs_s, o_win_s, o_conv_s, o_pool_s):
    ctx = ExitStack()
    with ctx:
        ctx.enter_context(nc.allow_non_contiguous_dma("small rows and relayouts"))
        base = (nc.sbuf_base + 31) // 32 * 32
        arena = ctx.enter_context(nc.sbuf_tensor("arena", [P, (206016 + 6368) // 4], F32))

        def at(name, shape, dt, off):
            return nc.alloc_sbuf_tensor_at(name, shape, dt, offset=base + off)

        def sems(*names):
            return [ctx.enter_context(nc.semaphore(n)) for n in names]

        dram = lambda name, shape, dt=F32: nc.dram_tensor(name, shape, dt, kind="Internal").ap()
        ab_dram = dram("compressed_halves", [DB, P, 2, 256])
        gate_dram = dram("sample_gates", [DB, 8, DS, 3])
        x1_dram = dram("layer0_out", [T, D])

        PS = ctx.enter_context(nc.psum_tensor("PS", [P, 8, 512], F32))

        XH = at("XH", [P, KT, T], F32R, 0)
        XL = at("XL", [P, KT, T], F32R, 33792)
        XHf, XLf = XH[:].bitcast(F32), XL[:].bitcast(F32)
        Q = at("Q", [P, 4, T], F32, 67584)
        BG = at("BG", [P, 4, T], F32, 84480)
        KV = at("KV", [P, 6, T], F32, 101376)
        U = at("U", [P, 4, UW + DB * US], F32, 126720)
        AG = [at(f"AG{i}", [P, T], F32, o) for i, o in enumerate((126720, 132032, 192480, 196704))]
        Y = at("Y", [P, 4, T], F32, 147936)
        WRAW = at("WRAW", [P, 2, KT, P], F32, 164832)
        WH = at("WH", [P, 2, KT, P], F32R, 173024)
        WL = at("WL", [P, 2, KT, P], F32R, 181216)
        SIG = at("SIG", [P, T], F32, 189408)
        CTMP = at("CTMP", [P, 8, 256], F32, 193632)
        AB = at("AB", [P, 2, 2, 256], F32, 201824)
        WB = at("WB", [P, 32, 256], F32, 67584)
        XC = at("XC", [P, 2, 2048], F32, 147936)
        XIN = at("XIN", [P, 3, D], F32, 101376)
        ROWS = at("ROWS", [34, 512], F32, 101376 + 12288)
        WCR = at("WCR", [32, 256], F32, 101376 + 14336)
        PSR = at("PSR", [8, P], F32, 101376 + 15360)
        STC = at("STC", [120, 2, 512], F32, 101376 + 15872)

        cur = [206016]

        def const(name, shape, dt=F32):
            n = int(np.prod(shape[1:])) * (2 if dt == BF16 else 4)
            t = at(name, shape, dt, cur[0])
            cur[0] += (n + 31) // 32 * 32
            return t

        ident = const("ident", [P, P])
        identb = const("identb", [P, P], BF16)
        mask_diag = const("mask_diag", [P, P], BF16)
        mask_far = const("mask_far", [P, P], BF16)
        mask_cmp = const("mask_cmp", [P, 120], BF16)
        meanm = const("meanm", [P, P])
        SM = const("SM", [P, 208])
        ULAST = const("ULAST", [P, 4, 62])
        idxf = const("idxf", [P, 40])
        idx = const("idx", [P, 32], I32)
        GTOK_AT = cur[0]
        GTOK = const("GTOK", [P, NTT, 24])
        KCT = const("KCT", [P, 2, 64])
        STAT = const("STAT", [P, 48])
        assert cur[0] <= 206016 + 6368, cur[0]
        VC = at("VC", [64, P], F32, 205408)
        CWT = SM[:, 0:136].rearrange("p (i k) -> p i k", i=4)
        WCT = SM[:, 136:200].rearrange("p (x j) -> p x j", x=2)
        PSC = SM[:, 200:208]
        (s_const, s_rows, s_pt, s_stc, s_idx, s_small, s_smalle, s_xt, s_xh, s_xl) = sems(
            "s_const", "s_rows", "s_pt", "s_stc", "s_idx", "s_small", "s_smalle", "s_xt", "s_xh", "s_xl")
        s_xin = sems("s_xin0", "s_xin1", "s_xin2")
        s_raw = sems("s_raw0", "s_raw1")
        s_xc = sems("s_xc0", "s_xc1")
        s_abst = sems("s_abst0", "s_abst1")
        (s_wb, s_wh, s_wl, s_mm, s_ev, s_u, s_xcfree, s_ab, s_cv, s_conv) = sems(
            "s_wb", "s_wh", "s_wl", "s_mm", "s_ev", "s_u", "s_xcfree", "s_ab", "s_cv", "s_conv")
        (s_tmt, s_tm, s_gt, s_gtok, s_ut, s_ue, s_kct, s_vct, s_vc, s_mean, s_yc, s_sq, s_sqr, s_yn, s_ys,
         s_ya, s_ah, s_al) = sems(
            "s_tmt", "s_tm", "s_gt", "s_gtok", "s_ut", "s_ue", "s_kct", "s_vct", "s_vc", "s_mean", "s_yc", "s_sq",
            "s_sqr", "s_yn", "s_ys", "s_ya", "s_ah", "s_al")
        (s_dve, s_pool, s_out, s_gd) = sems("s_dve", "s_pool", "s_out", "s_gd")
        outs = [0]

        xp_rows = x_prompt[0]
        xs_rows = x_sample.rearrange("b t d -> (b t) d")
        w_in = w_in_even[0].rearrange("(k p) e -> p k e", p=P)
        cmp_halves = cache_kv_cmp[0].rearrange("n (c h j) x g d -> (n c h) (j x g d)", c=8, h=2)
        sel_chunks = cache_kv_sel[0].rearrange("n (c j) x g d -> (n c) (j x g d)", c=8)

        UROW = at("UROW", [32, 2, 512], F32, 137344)
        G = at("G", [24, T], F32, 200928)
        (s_cs,) = sems("s_cs")
        CSUM = at("CSUM", [P, 4, NSAMP], F32, GTOK_AT)
        CTAP = at("CTAP", [P, 2, NSAMP], F32, GTOK_AT + 512)
        TM = at("TM", [P, NTT, 768], F32, 164832)

        def x_rows(tt):
            return xp_rows[tok(tt), :] if tt < NTT - 1 else xs_rows

        def mm_cols(m):
            if m < M_KV:
                o = (O_VAL, O_GLU)[m % 2] + (m // 2) * P
                return [(o, P)]
            if m < M_Q:
                return [(O_KV + (m - M_KV) * P, P)]
            if m < M_BG:
                g = m - M_Q
                return [(O_Q + g * HD, HD), (O_Q + (GROUP + g) * HD, HD)]
            if m < M_AG:
                g = m - M_BG
                return [(O_BG + g * HD, HD), (O_BG + (GROUP + g) * HD, HD)]
            if m < NM:
                return [(O_AG + (m - M_AG) * P, P)]
            return [(O_G, 24)]

        raw_need = {}
        cnt = [0, 0]
        for m in range(NM + 1):
            cnt[m % 2] += 16 * len(mm_cols(m))
            raw_need[m] = cnt[m % 2]

        def flat(banks):
            return banks.rearrange("p a c -> p (a c)")

        def samples(tile_cols):
            return tile_cols.rearrange("p (b t) -> p b t", b=DB)

        def sp_program(sp):
            sp.dma_start(ROWS[0:CW, :], conv_w[0]).then_inc(s_rows, 16)
            for r, v in enumerate((conv_b, conv_ln_g, conv_ln_b)):
                sp.dma_start(ROWS[CW + r:CW + r + 1, :], v).then_inc(s_rows, 16)
            sp.dma_start(WCR[:, :], w_cmp[0].rearrange("j x g d -> j (x g d)")).then_inc(s_rows, 16)
            sp.dma_start(PSR[:, :], pool_scale[0].rearrange("(i p) -> i p", p=P)).then_inc(s_rows, 16)
            for tt in range(3):
                sp.dma_start(XIN[:, tt, :], x_rows(tt)).then_inc(s_xin[tt], 16)
            sp.dma_start(STC[:, :, :], state_conv[0].rearrange("(a b) t c -> (b t) a c", a=2)).then_inc(s_stc, 16)
            for tt in range(3, NTT):
                sp.wait_ge(s_xt, 2 * (tt - 2))
                sp.dma_start(XIN[0:ntok(tt), tt % 3, :], x_rows(tt)).then_inc(s_xin[tt % 3], 16)
            sp.dma_start(WB[:, :, :], w_cmp[0].rearrange("j x g d -> (j x g d)").partition_broadcast(P)).then_inc(s_wb, 16)
            for b in range(DB):
                sp.wait_ge(s_ab, b + 1)
                sp.dma_start(ab_dram[b], AB[:, b % 2]).then_inc(s_abst[b % 2], 16)
            for dst, src in ((o_win_s[0, :, 0:WIN - DS], state_win_kv[0, :, DS:WIN]),
                             (o_conv_s[0, :, 0:CW - 1 - DS], state_conv[0, :, DS:CW - 1]),
                             (o_pool_s[0, :, 0:PMAX - 1 - DS], state_pool[0, :, DS:PMAX - 1])):
                sp.dma_start(dst, src).then_inc(s_out, 16)
                outs[0] += 16
            sp.wait_ge(s_tm, NTT)
            for dst, src in (
                    (o_kvc_p[0, 0], TM[:, 0:8, 0:256]), (o_kvs_p[0, 0], TM[:, 0:8, 256:512]),
                    (o_win_p[0, 0], TM[:, 4:8, 512:768])):
                sp.dma_start(dst.rearrange("(t p) x g d -> p t (x g d)", p=P), src).then_inc(s_out, 16)
                outs[0] += 16
            for dst, c in ((o_kvc_s, 0), (o_kvs_s, 256)):
                sp.dma_start(dst[0].rearrange("b t x g d -> (b t) (x g d)"), TM[0:NSAMP, 8, c:c + 256]).then_inc(s_vrow, 16)
            for b in range(DB):
                sp.dma_start(o_win_s[0, b, WIN - DS:WIN].rearrange("t x g d -> t (x g d)"),
                             TM[DS * b:DS * b + DS, 8, 512:768]).then_inc(s_vrow, 16)
            sp.wait_ge(s_ue, 2)
            sp.dma_start(o_conv_p[0, 0], UROW[0:CW - 1, 0, :]).then_inc(s_out, 16)
            outs[0] += 16
            for b in range(DB):
                sp.dma_start(o_conv_s[0, b, CW - 1 - DS:CW - 1], UROW[DS * b:DS * b + DS, 1, :]).then_inc(s_out, 16)
                outs[0] += 16
            sp.wait_ge(s_gtok, 1)
            for t in range(DS):
                sp.dma_start(gate_dram[:, :, t, :], GTOK[t:NSAMP:DS, 8, :].rearrange("p (g c) -> p g c", c=3)).then_inc(s_gd, 16)
            sp.wait_ge(s_vrow, 16 * (2 + DB))
            sp.wait_ge(s_gd, 16 * DS)
            sp.wait_ge(s_out, outs[0])
            sp.sem_inc(s_stored, 1)
            sp_late(sp)
            sp.wait_ge(s_out, outs[0])

        s_stored, s_vrow, s_varc, s_stdc = sems("s_stored", "s_vrow", "s_varc", "s_stdc")

        def load_w(sp, m):
            at_col = 0
            for c, n in mm_cols(m):
                sp.dma_start(WRAW[:, m % 2, :, at_col:at_col + n], w_in[:, :, c:c + n]).then_inc(s_raw[m % 2], 16)
                at_col += n

        def pool_program(po):
            k = [0]

            def link(ins):
                k[0] += 1
                ins.then_inc(s_pool, 1)
                po.wait_ge(s_pool, k[0])

            for r in range(8):
                po.dma_start(idx[r::8, 0:8], page_table.rearrange("b n -> n b")).then_inc(s_pt, 16)
            link(po.memset(ident[:, :], 0.0))
            po.affine_select(out=ident[:, :], in_=ident[:, :], compare_op=ALU.not_equal, fill=1.0, base=0,
                             pattern=[[-1, P]], channel_multiplier=1).then_inc(s_const, 1)
            link(po.iota(idx[:, 24:25], pattern=[[0, 1]], base=0, channel_multiplier=1))
            po.memset(meanm[:, :], 1.0 / WC).then_inc(s_const, 1)
            link(po.memset(mask_diag[:, :], 0.0))
            link(po.affine_select(out=mask_diag[:, :], in_=mask_diag[:, :], compare_op=ALU.is_ge, fill=NEG, base=0,
                                  pattern=[[-1, P]], channel_multiplier=1))
            link(po.memset(mask_far[:, :], 0.0))
            link(po.affine_select(out=mask_far[:, :], in_=mask_far[:, :], compare_op=ALU.is_ge, fill=NEG, base=-1,
                                  pattern=[[1, P]], channel_multiplier=-1))
            link(po.memset(mask_cmp[:, :], 0.0))
            link(po.affine_select(out=mask_cmp[:, :], in_=mask_cmp[:, :], compare_op=ALU.is_ge, fill=NEG,
                                  base=CSTR * 56 - 2 * CSTR + 1, pattern=[[-CSTR, 120]], channel_multiplier=1))
            po.wait_ge(s_const, 2)
            po.tensor_copy(identb[:, :], ident[:, :]).then_inc(s_const, 1)

            def gather(n):
                b, hf = n // 2, n % 2
                if n >= 2:
                    po.wait_ge(s_xcfree, n - 1)
                o = 8 + 8 * hf + b
                po.indirect_dma_start(out=XC[:, n % 2, :], out_offset=None, in_=cmp_halves,
                                      in_offset=bass.IndirectOffsetOnAxis(ap=idx[:, o:o + 1], axis=0))\
                    .then_inc(s_xc[n % 2], 16)

            def conv_samples(t):
                if t == 0:
                    po.wait_ge(s_u, 4)
                for a in range(2):
                    dst = CSUM[:, 2 * a:2 * a + 2, :].rearrange("p i (b t) -> p i b t", b=DB)
                    tmp = (CTAP if t else CSUM[:, 2 * a:2 * a + 2, :])[:, :, :].rearrange("p i (b t) -> p i b t", b=DB)
                    src = U[:, 2 * a:2 * a + 2, UW:].rearrange("p i (b t) -> p i b t", b=DB)[:, :, :, t:t + DS]
                    w = CWT[:, 2 * a:2 * a + 2, t:t + 1].unsqueeze(3).to_broadcast([P, 2, DB, DS])
                    link(po.tensor_tensor(tmp, src, w, ALU.mult))
                    if t == 0:
                        tmp = CWT[:, 2 * a:2 * a + 2, CW:CW + 1].unsqueeze(3).to_broadcast([P, 2, DB, DS])
                    link(po.tensor_tensor(dst, dst, tmp, ALU.add))

            po.wait_ge(s_idx, 1)
            gather(0)
            gather(1)
            for m in range(NM + 1):
                po.wait_ge(s_wh, m + 1)
                n = 24 if m == NM else P
                po.tensor_tensor(WL[:, m % 2, :, 0:n], WRAW[:, m % 2, :, 0:n], WH[:, m % 2, :, 0:n].bitcast(F32),
                                 ALU.subtract).then_inc(s_wl, 1)
                if 1 <= m and m + 1 < 2 * DB:
                    gather(m + 1)
                if m > M_KV:
                    for t in range(3 * (m - M_KV - 1), min(CW, 3 * (m - M_KV))):
                        conv_samples(t)
                if 3 * (m - M_KV) == 3 * -(-CW // 3):
                    po.sem_inc(s_cs, 1)
            for i in range(4):
                po.wait_ge(s_ys, i + 1)
                po.tensor_tensor(Y[:, i, :], Y[:, i, :], AG[i][:, :], ALU.mult).then_inc(s_ya, 1)
            pool_late(po, link)

        def act_program(act):
            load_w(act, 0)
            load_w(act, 1)
            for tt in range(NTT):
                for hf in range(2):
                    act.wait_ge(s_xt, 2 * tt + hf + 1)
                    act.activation(XH[:, 4 * hf:4 * hf + 4, tok(tt)],
                                   PS[:, 2 * (tt % 2) + hf, :].rearrange("p (k t) -> p k t", k=4)[:, :, 0:ntok(tt)],
                                   ACT.Copy).then_inc(s_xh, 1)

            def high(m):
                act.wait_ge(s_raw[m % 2], raw_need[m])
                if m >= 2:
                    act.wait_ge(s_mm, m - 1)
                n = 24 if m == NM else P
                act.activation(WH[:, m % 2, :, 0:n], WRAW[:, m % 2, :, 0:n], ACT.Copy).then_inc(s_wh, 1)

            def evac(m):
                b0 = 3 * (m % 2)
                three = PS[:, b0:b0 + 3, 0:CH]
                act.wait_ge(s_mm, m + 1)
                if m < M_KV and m % 2 == 0:
                    i = m // 2
                    act.activation(U[:, i, CW - 1:CW - 1 + 2 * CH].rearrange("p (a c) -> p a c", a=2),
                                   PS[:, b0:b0 + 2, 0:CH], ACT.Copy)
                    act.activation(U[:, i, CW - 1 + 2 * CH:UW], PS[:, b0 + 2, 0:SEQ - 2 * CH], ACT.Copy)
                    act.activation(samples(U[:, i, UW:])[:, :, CW - 1:US],
                                   PS[:, b0 + 2, SEQ - 2 * CH:CH].rearrange("p (b t) -> p b t", b=DB),
                                   ACT.Copy).then_inc(s_ev, 1)
                    return
                if m < M_KV:
                    out, f = SIG[:, :], ACT.Sigmoid
                    if m >= 3:
                        act.wait_ge(s_u, m // 2)
                elif m < M_Q:
                    out, f = KV[:, m - M_KV, :], ACT.Copy
                elif m < M_BG:
                    act.wait_ge(s_ab, DB)
                    out, f = Q[:, m - M_Q, :], ACT.Copy
                elif m < M_AG:
                    out, f = BG[:, m - M_BG, :], ACT.Silu
                elif m < NM:
                    i = m - M_AG
                    if i < 2:
                        act.wait_ge(s_cs, 1)
                        act.wait_ge(s_conv, i + 1)
                    else:
                        act.wait_ge(s_kct, 2)
                    out, f = AG[i][:, :], ACT.Silu
                else:
                    act.wait_ge(s_kct, 2)
                    out, f = G[:, :], ACT.Sigmoid
                    three = PS[0:24, b0:b0 + 3, 0:CH]
                act.activation(out.rearrange("p (a c) -> p a c", a=3), three, f).then_inc(s_ev, 1)

            high(0)
            high(1)
            for m in range(NM + 1):
                evac(m)
                if m + 2 <= NM:
                    act.wait_ge(s_wl, m + 1)
                    load_w(act, m + 2)
                    high(m + 2)
            for tt in range(NTT):
                act.wait_ge(s_tmt, tt + 1)
                n, b0 = ntok(tt), (3, 6)[tt % 2]
                act.activation(TM[0:n, tt, :], flat(PS[0:n, b0:b0 + 2, :])[:, 0:768], ACT.Copy).then_inc(s_tm, 1)
            for i in range(4):
                act.wait_ge(s_yc, 1)
                if i >= 2:
                    act.wait_ge(s_sqr, i - 1)
                if i == 0:
                    act.wait_ge(s_kct, 2)
                act.activation(KV[:, i % 2, :], Y[:, i, :], ACT.Square).then_inc(s_sq, 1)
            act.wait_ge(s_varc, 1)
            act.activation(KV[:, 3, :], KV[:, 3, :], ACT.Sqrt).then_inc(s_stdc, 1)
            for i in range(4):
                act.wait_ge(s_yn, i + 1)
                act.activation(Y[:, i, :], Y[:, i, :], ACT.Silu, bias=CWT[:, i, 33:34], scale=CWT[:, i, 32:33])\
                    .then_inc(s_ys, 1)
            for i in range(4):
                act.wait_ge(s_ya, i + 1)
                act.activation(XH[:, i, :], Y[:, i, :], ACT.Copy).then_inc(s_ah, 1)
            act_late(act)

        def dve_program(v):
            k = [0]

            def link(ins):
                k[0] += 1
                ins.then_inc(s_dve, 1)
                v.wait_ge(s_dve, k[0])

            v.sem_inc(s_ev, 2)
            v.memset(U[:, :, 0:CW - 1], 0.0)
            v.wait_ge(s_pt, 16 * 8)
            link(v.tensor_copy(idxf[:, 0:8], idx[:, 0:8]))
            v.wait_ge(s_pool, 2)
            link(v.tensor_scalar(idx[:, 25:26], idx[:, 24:25], 7, None, ALU.bitwise_and))
            link(v.tensor_copy(idxf[:, 9:10], idx[:, 25:26]))
            link(v.tensor_scalar(idxf[:, 10:11], idxf[:, 9:10], 2.0, None, ALU.mult))
            v.tensor_scalar(idxf[:, 16:24], idxf[:, 0:8], 16.0, idxf[:, 10:11], ALU.mult, ALU.add)
            link(v.tensor_scalar(idxf[:, 32:40], idxf[:, 0:8], 8.0, idxf[:, 9:10], ALU.mult, ALU.add))
            link(v.tensor_scalar(idxf[:, 24:32], idxf[:, 16:24], 1.0, None, ALU.add))
            v.tensor_copy(idx[:, 8:32], idxf[:, 16:40]).then_inc(s_idx, 1)
            v.wait_ge(s_small, 1)
            v.tensor_copy(SM[:, :], PS[:, 7, 0:208]).then_inc(s_smalle, 1)
            for a in range(2):
                v.wait_ge(s_small, 2 + a)
                for i in range(4):
                    v.tensor_copy(samples(U[:, i, UW:])[:, 4 * a:4 * a + 4, 0:CW - 1],
                                  PS[:, 6 - a, 120 * i:120 * i + 120].rearrange("p (b t) -> p b t", b=4))
            for tt in range(NTT):
                for hf in range(2):
                    n = 2 * tt + hf
                    v.wait_ge(s_xh, n + 1)
                    v.tensor_tensor(XL[:, 4 * hf:4 * hf + 4, tok(tt)],
                                    PS[:, 2 * (tt % 2) + hf, :].rearrange("p (k t) -> p k t", k=4)[:, :, 0:ntok(tt)],
                                    XHf[:, 4 * hf:4 * hf + 4, tok(tt)], ALU.subtract).then_inc(s_xl, 1)

            def glu(i):
                v.wait_ge(s_ev, 2 + 2 * i + 2)
                v.tensor_tensor(U[:, i, CW - 1:UW], U[:, i, CW - 1:UW], SIG[:, 0:SEQ], ALU.mult)
                us = samples(U[:, i, UW:])[:, :, CW - 1:US]
                link(v.tensor_tensor(us, us, SIG[:, SEQ:T].rearrange("p (b t) -> p b t", b=DB), ALU.mult))
                v.tensor_copy(ULAST[:, i, 0:CW - 1], U[:, i, SEQ:UW])
                v.tensor_copy(ULAST[:, i, CW - 1:].rearrange("p (b t) -> p b t", b=DB), us).then_inc(s_u, 1)

            def compress(n):
                b, hf = n // 2, n % 2
                v.wait_ge(s_xc[n % 2], 16 * (n // 2 + 1))
                if n == 0:
                    v.wait_ge(s_wb, 16)
                if b >= 2 and hf == 0:
                    v.wait_ge(s_abst[b % 2], 16 * (b // 2))
                x3 = XC[:, n % 2, :].rearrange("p (j c) -> p j c", j=8)
                for w in range(2):
                    ins = v.tensor_tensor(CTMP[:, :, :], x3, WB[:, 16 * w + 8 * hf:16 * w + 8 * hf + 8, :], ALU.mult)
                    link(ins)
                    if hf:
                        link(v.tensor_tensor(CTMP[:, 0, :], CTMP[:, 0, :], AB[:, b % 2, w, :], ALU.add))
                    ins = v.tensor_reduce(AB[:, b % 2, w, :], CTMP[:, :, :].rearrange("p j c -> p c j"), AX, ALU.add)
                    link(ins)
                v.sem_inc(s_xcfree, 1)
                if hf:
                    v.sem_inc(s_ab, 1)

            for m in range(NM):
                if m < M_KV and m % 2:
                    glu(m // 2)
                if m < 2 * DB:
                    compress(m)
            v.wait_ge(s_ev, 2 + M_KV + 2)
            v.wait_ge(s_abst[0], 16 * DB // 2)
            v.wait_ge(s_abst[1], 16 * DB // 2)
            for x in range(2):
                for w in range(2):
                    link(v.tensor_tensor(CTMP[:, 0:4, :].rearrange("p a c -> p (a c)").rearrange("p (n j) -> p n j", j=CSTR),
                                         KV[:, x, 0:SEQ].rearrange("p (n j) -> p n j", j=CSTR),
                                         WCT[:, x, 16 * w:16 * w + 16].unsqueeze(1).to_broadcast([P, SEQ // CSTR, CSTR]),
                                         ALU.mult))
                    link(v.tensor_reduce(AB[:, 0, 0, 64 * w:64 * w + 64],
                                         CTMP[:, 0:4, :].rearrange("p a c -> p (a c)").rearrange("p (n j) -> p n j", j=CSTR),
                                         AX, ALU.add))
                v.tensor_tensor(KCT[:, x, 0:NCP], AB[:, 0, 0, 0:NCP], AB[:, 0, 0, 65:128], ALU.add).then_inc(s_kct, 1)
                v.wait_ge(s_kct, x + 1)
            c = 0
            for pair in range(2):
                for t in range(CW):
                    for i in (2 * pair, 2 * pair + 1):
                        src, dst = U[:, i, t:t + SEQ], Y[:, i, 0:SEQ]
                        if t:
                            v.wait_ge(s_cv, c - 1)
                        if t == 0:
                            ins = v.tensor_scalar(dst, src, CWT[:, i, 0:1], CWT[:, i, CW:CW + 1], ALU.mult, ALU.add)
                        else:
                            ins = v.scalar_tensor_tensor(dst, src, CWT[:, i, t:t + 1], dst, ALU.mult, ALU.add)
                        ins.then_inc(s_cv, 1)
                        c += 1
                v.wait_ge(s_cv, c)
                if pair == 0:
                    v.sem_inc(s_conv, 2)
            v.wait_ge(s_cs, 1)
            v.tensor_copy(Y[:, :, SEQ:T], CSUM[:, :, :]).then_inc(s_conv, 2)
            v.wait_ge(s_conv, 4)
            v.wait_ge(s_gt, 1)
            v.tensor_copy(GTOK[:, 0:8, :], PS[:, 5, 0:192].rearrange("p (t g) -> p t g", g=24))
            v.tensor_copy(GTOK[0:NSAMP, 8, :], PS[0:NSAMP, 5, 192:216]).then_inc(s_gtok, 1)
            v.wait_ge(s_ut, 1)
            v.tensor_copy(UROW[0:CW - 1, 0, :], PS[0:CW - 1, 0, :]).then_inc(s_ue, 1)
            v.tensor_copy(UROW[:, 1, :], PS[0:NSAMP, 1, :]).then_inc(s_ue, 1)
            v.wait_ge(s_vct, 1)
            v.tensor_copy(VC[0:NCP, :], PS[0:NCP, 2, 0:P]).then_inc(s_vc, 1)
            v.wait_ge(s_mean, 1)
            for i in range(4):
                ins = v.tensor_tensor(Y[:, i, :].rearrange("p (a c) -> p a c", a=3),
                                      Y[:, i, :].rearrange("p (a c) -> p a c", a=3), PS[:, 0:3, 0:CH], ALU.subtract)
            ins.then_inc(s_yc, 1)
            v.wait_ge(s_sqr, 4)
            v.tensor_scalar(KV[:, 3, :].rearrange("p (a c) -> p a c", a=3), PS[:, 3:6, 0:CH], EPS, None,
                            ALU.add).then_inc(s_varc, 1)
            v.wait_ge(s_stdc, 1)
            link(v.reciprocal(KV[:, 3, :], KV[:, 3, :]))
            for i in range(4):
                v.tensor_tensor(Y[:, i, :], Y[:, i, :], KV[:, 3, :], ALU.mult).then_inc(s_yn, 1)
            for i in range(4):
                v.wait_ge(s_ah, i + 1)
                v.tensor_tensor(XL[:, i, :], Y[:, i, :], XHf[:, i, :], ALU.subtract).then_inc(s_al, 1)
            dve_late(v, link)

        def pe_program(pe):
            pe.wait_ge(s_const, 3)
            pe.wait_ge(s_rows, 16 * 6)
            for i in range(4):
                pe.transpose(PS[:, 7, 34 * i:34 * i + 34], ROWS[:, i * P:i * P + P], ident[0:34, 0:34])
            for x in range(2):
                pe.transpose(PS[:, 7, 136 + 32 * x:168 + 32 * x], WCR[:, x * P:x * P + P], ident[0:32, 0:32])
            pe.transpose(PS[:, 7, 200:208], PSR[:, :], ident[0:8, 0:8]).then_inc(s_small, 1)
            pe.wait_ge(s_stc, 16)
            for a in range(2):
                for i in range(4):
                    ins = pe.transpose(PS[:, 6 - a, 120 * i:120 * i + 120], STC[:, a, i * P:i * P + P], ident[0:120, 0:120])
                ins.then_inc(s_small, 1)
            for tt in range(NTT):
                n = ntok(tt)
                pe.wait_ge(s_xin[tt % 3], 16 * (tt // 3 + 1))
                for hf in range(2):
                    if tt >= 2:
                        pe.wait_ge(s_xl, 2 * (tt - 2) + hf + 1)
                    for j in range(4):
                        ins = pe.transpose(PS[:, 2 * (tt % 2) + hf, j * P:j * P + n],
                                           XIN[0:n, tt % 3, (4 * hf + j) * P:(4 * hf + j + 1) * P], ident[0:n, 0:n])
                    ins.then_inc(s_xt, 1)
            pe.wait_ge(s_xl, 2 * NTT)
            pe.wait_ge(s_smalle, 1)

            def product(slot, mcols):
                b0 = 3 * slot
                for kk in range(KT):
                    for n, (w, x) in enumerate(((WH, XH), (WH, XL), (WL, XH))):
                        for c in range(3):
                            ins = pe.matmul(PS[0:mcols, b0 + c, 0:CH], w[:, slot, kk, 0:mcols], x[:, kk, c * CH:(c + 1) * CH],
                                            start=(kk == 0 and n == 0), stop=(kk == KT - 1 and n == 2))
                return ins

            with pe.Fori(0, NM // 2) as pair:
                for slot in range(2):
                    pe.wait_ge(s_wl, pair * 2 + (slot + 1))
                    pe.wait_ge(s_ev, pair * 2 + (slot + 1))
                    product(slot, P).then_inc(s_mm, 1)
            pe.wait_ge(s_wl, NM + 1)
            pe.wait_ge(s_ev, NM + 1)
            product(0, 24).then_inc(s_mm, 1)
            for tt in range(NTT):
                n, b0 = ntok(tt), (3, 6)[tt % 2]
                if tt == 0:
                    pe.wait_ge(s_ev, NM + 2)
                if tt >= 2:
                    pe.wait_ge(s_tm, tt - 1)
                for x in range(6):
                    ins = pe.transpose(PS[0:n, b0 + x // 4, (x % 4) * P:(x % 4) * P + P], KV[:, x, tok(tt)], ident[:, :])
                ins.then_inc(s_tmt, 1)
            pe.wait_ge(s_ev, NM + 3)
            for tt in range(NTT):
                n = ntok(tt)
                ins = pe.transpose(PS[0:n, 5, 24 * tt:24 * tt + 24], G[:, tok(tt)], ident[0:24, 0:24])
            ins.then_inc(s_gt, 1)
            pe.wait_ge(s_u, 4)
            for i in range(4):
                pe.transpose(PS[0:CW - 1, 0, i * P:i * P + P], ULAST[:, i, 0:CW - 1], ident[:, :])
                ins = pe.transpose(PS[0:NSAMP, 1, i * P:i * P + P], ULAST[:, i, CW - 1:], ident[:, :])
            ins.then_inc(s_ut, 1)
            pe.wait_ge(s_kct, 2)
            pe.transpose(PS[0:NCP, 2, 0:P], KCT[:, 1, 0:NCP], ident[:, :]).then_inc(s_vct, 1)
            pe.wait_ge(s_ue, 2)
            pe.wait_ge(s_vc, 1)
            pe.wait_ge(s_conv, 4)
            for i in range(4):
                for c in range(3):
                    ins = pe.matmul(PS[:, c, 0:CH], meanm[:, :], Y[:, i, c * CH:(c + 1) * CH], start=(i == 0), stop=(i == 3))
            ins.then_inc(s_mean, 1)
            pe.wait_ge(s_gtok, 1)
            pe.wait_ge(s_tm, NTT)
            for i in range(4):
                pe.wait_ge(s_sq, i + 1)
                for c in range(3):
                    ins = pe.matmul(PS[:, 3 + c, 0:CH], meanm[:, :], KV[:, i % 2, c * CH:(c + 1) * CH], start=(i == 0), stop=(i == 3))
                ins.then_inc(s_sqr, 1)
            pe_late(pe)

        (s_sc, s_nm, s_exp, s_rc, s_scl, s_tpt, s_pted, s_ptea, s_pv, s_om, s_oh, s_ol) = sems(
            "s_sc", "s_nm", "s_exp", "s_rc", "s_scl", "s_tpt", "s_pted", "s_ptea", "s_pv", "s_om", "s_oh", "s_ol")
        PRS = at("PRS", [P, GROUP, SEQ], F32, 126720)
        PRW = at("PRW", [P, GROUP, WIN + P], F32, 143104)
        PRC = at("PRC", [P, GROUP, 64], F32, 153344)
        PT = at("PT", [P, 2, 512], F32, 159488)
        OT = at("OT", [P, 2, 512], F32, 193632)
        NMX, DEN, RCP, MXS = (STAT[:, 12 * i:12 * i + 12] for i in range(4))
        CMPB, SELBR, WINB = 0, 1, 2
        UNITS = [(qt, h, br) for qt in range(SEQ // P) for h in range(2) for br in (SELBR, WINB, CMPB)]

        def key_tiles(u):
            qt, _, br = UNITS[u]
            return {SELBR: list(range(qt + 1)), WINB: list(range(max(0, qt - 4), qt + 1)), CMPB: [0]}[br]

        def nkeys(u):
            return NCP if UNITS[u][2] == CMPB else P * len(key_tiles(u))

        def probs(j, k0, n):
            return {SELBR: PRS, WINB: PRW, CMPB: PRC}[UNITS[j // 4][2]][:, j % 4, k0:k0 + n]

        ORDER = []
        turn_unit, unit_last_turn, scores_end = [], {}, {}
        todo = [(u, i) for u in range(len(UNITS)) for i in range(len(key_tiles(u)))]
        col, job, since, later = 0, 0, 0, []
        LAG, NJ = 3500, 4 * len(UNITS)
        while job < NJ or todo:
            u, i = todo[0] if todo else (len(UNITS), 0)
            slot_free = job < NJ and (job // 4 < 3 or job // 4 - 3 < u)
            ready = (todo and u in scores_end and (job == NJ or job >= 4 * u + 6)
                     and (col - scores_end[u] >= LAG or not slot_free))
            if ready and (since < 2 or not slot_free):
                ORDER.append(("T", len(turn_unit), u, i))
                turn_unit.append(u)
                unit_last_turn[u] = len(turn_unit) - 1
                todo.pop(0)
                col += 1024
                since += 1
                turned_branch = UNITS[u][2] == CMPB
            else:
                ORDER.append(("S", job))
                col += nkeys(job // 4) + P
                if job % 4 == 3:
                    scores_end[job // 4] = col
                job += 1
                since = 0
                turned_branch = False
                if job == NJ:
                    ORDER.append(("R",))
            ORDER += later[:1]
            later = later[1:]
            if turned_branch:
                later += [("-",), ("-",), ("-",), ("O", u // 3), ("L", u // 3)]
        ORDER += [("F",)] + later
        NT = len(turn_unit)

        score_bank, bank_waits, holder, nxt = [], [], {}, 0
        for j in range(NJ):
            n = -(-nkeys(j // 4) // 512)
            nxt = (nxt + n - 1) // n * n % 4
            bank_waits.append(max(holder.get(nxt + i, -1) for i in range(n)))
            score_bank.append(nxt)
            for i in range(n):
                holder[nxt + i] = j
            nxt = (nxt + n) % 4

        def evac_count(t):
            return (s_pted, t // 2 + 1) if t % 2 == 0 else (s_ptea, t // 2 + 1)

        def pe_attention(pe):
            pending = [None]

            def values(t, u, i):
                qt, h, br = UNITS[u]
                hb = HD * h
                pe.wait_ge(*evac_count(t))
                first = br == SELBR and i == 0
                n = 2 * qt + h
                if first and n >= 2:
                    pe.wait_ge(s_om, n - 1)
                kt = key_tiles(u)[i]
                v, rows = {SELBR: (TM[:, kt, 384 + hb:384 + hb + HD], P), WINB: (TM[:, kt, 640 + hb:640 + hb + HD], P),
                           CMPB: (VC[0:NCP, hb:hb + HD], NCP)}[br]
                pe.matmul(PS[hb:hb + HD, 6 + h, :], v, PT[0:rows, t % 2, :], start=first,
                          stop=(br == CMPB)).then_inc(s_pv, 1)

            def flush():
                if pending[0]:
                    values(*pending[0])
                pending[0] = None

            pe.wait_ge(s_varc, 1)
            pe.wait_ge(s_yc, 1)
            for ev in ORDER:
                if ev[0] == "S":
                    j = ev[1]
                    u, g = j // 4, j % 4
                    qt, h, br = UNITS[u]
                    hb, b0 = HD * h, score_bank[j]
                    if bank_waits[j] >= 0:
                        pe.wait_ge(s_exp, bank_waits[j] + 1)
                    keys = {SELBR: KV[hb:hb + HD, 2, :], WINB: KV[hb:hb + HD, 4, :], CMPB: KCT[hb:hb + HD, 0, :]}[br]
                    k0 = P * key_tiles(u)[0]
                    q = Q[hb:hb + HD, g, tok(qt)]
                    nk = nkeys(u)
                    masks = []
                    if br == CMPB:
                        masks.append((0, mask_cmp[:, 56 - 8 * qt:56 - 8 * qt + NCP]))
                    else:
                        masks.append((nk - P, mask_diag[:, :]))
                        if br == WINB and qt >= 4:
                            masks.append((0, mask_far[:, :]))
                    for b in range(0, nk, 512):
                        w = min(512, nk - b)
                        mine = [(o, m) for o, m in masks if b <= o < b + w]
                        ins = pe.matmul(PS[:, b0 + b // 512, 0:w], q, keys[:, k0 + b:k0 + b + w], start=True, stop=True)
                        for o, m in mine:
                            ins = pe.matmul(PS[:, b0 + b // 512, o - b:o - b + m.shape[1]], identb[:, :], m,
                                            start=False, stop=True, skip_group_check=True)
                    ins.then_inc(s_sc, 1)
                    flush()
                elif ev[0] == "T":
                    _, t, u, i = ev
                    pe.wait_ge(s_scl, 4 * u + 4)
                    if t >= 2:
                        pe.wait_ge(*evac_count(t - 2))
                    cols = NCP if UNITS[u][2] == CMPB else P
                    for g in range(GROUP):
                        ins = pe.transpose(PS[0:cols, 4 + t % 2, g * P:g * P + P],
                                           probs(4 * u + g, i * P, cols), ident[:, :])
                    ins.then_inc(s_tpt, 1)
                    flush()
                    pending[0] = (t, u, i)
                elif ev[0] == "F":
                    flush()

        def scores_of(j):
            n = nkeys(j // 4)
            return flat(PS[:, score_bank[j]:score_bank[j] + -(-n // 512), :])[:, 0:n]

        def evacuate_turn(eng, copy, t, u, sem):
            eng.wait_ge(s_tpt, t + 1)
            if t >= 2:
                eng.wait_ge(s_pv, t - 1)
            rows = NCP if UNITS[u][2] == CMPB else P
            copy(PT[0:rows, t % 2, :], PS[0:rows, 4 + t % 2, :]).then_inc(sem, 1)

        def out_slices(n):
            qt, h = n // 2, n % 2
            hb = HD * h
            o = OT[hb:hb + HD, qt % 2, :].rearrange("p (g t) -> p g t", g=GROUP)
            return qt, h, hb, o

        def act_attention(act):
            act.wait_ge(s_al, 4)
            act.wait_ge(s_stored, 1)

            def exponential(j):
                act.wait_ge(s_nm, j + 1)
                if j >= 12:
                    act.wait_ge(s_tpt, unit_last_turn[j // 4 - 3] + 1)
                act.activation(probs(j, 0, nkeys(j // 4)), scores_of(j), ACT.Exp, bias=NMX[:, j % 12:j % 12 + 1],
                               scale=SCALE, accum_out=DEN[:, j % 12:j % 12 + 1]).then_inc(s_exp, 1)

            for ev in ORDER:
                if ev[0] == "S" and ev[1]:
                    exponential(ev[1] - 1)
                elif ev[0] == "R":
                    exponential(NJ - 1)
                elif ev[0] == "T" and ev[1] % 2:
                    evacuate_turn(act, lambda o, i: act.activation(o, i, ACT.Copy), ev[1], ev[2], s_ptea)
                elif ev[0] == "O":
                    qt, h, hb, o = out_slices(ev[1])
                    act.wait_ge(s_om, ev[1] + 1)
                    act.activation(XH[hb:hb + HD, 4:8, tok(qt)], o, ACT.Copy).then_inc(s_oh, 1)

        def dve_attention(v, link):
            def recip(j):
                v.wait_ge(s_exp, j + 1)
                d = DEN[:, j % 12:j % 12 + 1]
                if UNITS[j // 4][2] == CMPB:
                    link(v.tensor_scalar(d, d, 1e-30, None, ALU.max))
                v.reciprocal(RCP[:, j % 12:j % 12 + 1], d).then_inc(s_rc, 1)

            for ev in ORDER:
                if ev[0] == "S":
                    j = ev[1]
                    v.wait_ge(s_sc, j + 1)
                    link(v.tensor_reduce(MXS[:, j % 12:j % 12 + 1], scores_of(j), AX, ALU.max))
                    v.tensor_scalar(NMX[:, j % 12:j % 12 + 1], MXS[:, j % 12:j % 12 + 1], -1e28, -SCALE, ALU.max,
                                    ALU.mult).then_inc(s_nm, 1)
                    if j >= 2:
                        recip(j - 2)
                elif ev[0] == "R":
                    recip(NJ - 2)
                    recip(NJ - 1)
                elif ev[0] == "T":
                    if ev[1] % 2 == 0:
                        evacuate_turn(v, v.tensor_copy, ev[1], ev[2], s_pted)
                elif ev[0] == "O":
                    qt, h, hb, o = out_slices(ev[1])
                    n = ev[1]
                    if n == 8:
                        dve_sample_halves(v)
                    v.wait_ge(s_pv, unit_last_turn[3 * n + 2] + 1)
                    v.tensor_tensor(o, PS[hb:hb + HD, 6 + h, :].rearrange("p (g t) -> p g t", g=GROUP),
                                    BG[hb:hb + HD, :, tok(qt)], ALU.mult).then_inc(s_om, 1)
                elif ev[0] == "L":
                    qt, h, hb, o = out_slices(ev[1])
                    v.wait_ge(s_oh, ev[1] + 1)
                    v.tensor_tensor(XL[hb:hb + HD, 4:8, tok(qt)], o, XHf[hb:hb + HD, 4:8, tok(qt)],
                                    ALU.subtract).then_inc(s_ol, 1)

        def pool_attention(po):
            po.wait_ge(s_gtok, 1)
            for j in range(4 * len(UNITS)):
                qt, h, br = UNITS[j // 4]
                c = (GROUP * h + j % 4) * 3 + br
                po.wait_ge(s_rc, j + 1)
                p = probs(j, 0, nkeys(j // 4))
                po.tensor_scalar(p, p, RCP[:, j % 12:j % 12 + 1], GTOK[:, qt, c:c + 1], ALU.mult, ALU.mult)\
                    .then_inc(s_scl, 1)

        QBD = at("QBD", [P, DB, 32], F32, 122496)
        BGS = at("BGS", [P, 4, NSAMP], F32, 123520)
        KN = at("KN", [P, 2, NSAMP], F32, 124032)
        SE = at("SE", [P, 64], F32, 124320)
        GR = SE[:, 0:6].rearrange("p (a c) -> p a c", a=2)
        TCOL = SE[:, 6:7]
        C4 = SE[:, 7:11]
        NM4 = SE[:, 11:15]
        WM4 = SE[:, 15:19]
        SNEW = SE[:, 19:27]
        EMX, ENM, EDN, ERC = (SE[:, 27 + 4 * i:31 + 4 * i] for i in range(4))
        TI = at("TI", [P, 8], I32, 124320 + 256)
        KCA = at("KCA", [P, DB, 256], F32, 101376)
        KCB = [at("KCB0", [P, 4, 256], F32, 114048), at("KCB1", [P, 4, 256], F32, 154368)]
        WCA = at("WCA", [P, 4, 4, 256], F32, 75776)
        KCTS = at("KCTS", [P, DB, P], F32, 111200)
        PC = at("PC", [P, 2, P], F32, 115328)
        M32 = at("M32", [P, 2, 32], F32, 116352)
        CNT = at("CNT", [P, 2, 32], F32, 116608)
        SCR = at("SCR", [P, 2, 32], F32, 116864)
        M128 = at("M128", [P, 2, P], F32, 117120)
        PTC = at("PTC", [P, 2, P], F32, 118144)
        LT = at("LT", [P, NFREE, NFREE], F32, 92160)
        RG = at("RG", [P, NFREE, NFREE], F32, 95776)
        RE = at("RE", [P, NFREE, NFREE], F32, 200448)
        SS = at("SS", [P, PAST + DS], F32, 92160)
        VN = at("VN", [DS, 2, DB, P], F32, 67584)
        KTW = at("KTW", [P, 512], F32, 111200)
        SW = at("SW", [P, WIN + DS], F32, 113248)
        PTW = at("PTW", [P, 4, 64], F32, 109568)
        PTN = at("PTN", [DS, 2, 64], F32, 110592)
        OS = at("OS", [P, 2, P], F32, 119168)
        GSM = at("GSM", [P, P], F32, 120192)
        O2 = at("O2", [P, 2, 64], F32, 100384)
        RING = at("RING", [P, 4, 4096], F32, 126720)
        KTS = at("KTS", [P, PAST], F32, 192256)
        PTS = at("PTS", [P, 16, 64], F32, 200448)
        (s_qbd, s_kab, s_vn, s_gr, s_wc0, s_wc1, s_wc2, s_wc3, s_kc, s_kct2, s_kct2e, s_csc, s_cnm, s_cex, s_pcn, s_gsm, s_gs, s_m,
         s_pcg, s_pct, s_ptc, s_tg, s_tgv, s_tga, s_ksc, s_ss, s_enm, s_eex, s_erc, s_esc, s_pvb, s_os, s_o2, s_o2h,
         s_lt, s_gsm2) = sems(
            "s_qbd", "s_kab", "s_vn", "s_gr", "s_wc0", "s_wc1", "s_wc2", "s_wc3", "s_kc", "s_kct2", "s_kct2e", "s_csc", "s_cnm", "s_cex",
            "s_pcn", "s_gsm", "s_gs", "s_m", "s_pcg", "s_pct", "s_ptc", "s_tg", "s_tgv", "s_tga", "s_ksc", "s_ss",
            "s_enm", "s_eex", "s_erc", "s_esc", "s_pvb", "s_os", "s_o2", "s_o2h", "s_lt", "s_gsm2")
        s_wc = [s_wc0, s_wc1, s_wc2, s_wc3]
        s_ring = sems("s_ring0", "s_ring1", "s_ring2", "s_ring3")

        EV = []
        tiles_of = {}

        def put(*ev, turned=False):
            EV.append(ev)
            if turned:
                tiles_of[ev] = len(tiles_of)

        for gi in range(5):
            if gi < 4:
                for b in (2 * gi, 2 * gi + 1):
                    for i in range(5):
                        put("kt", b, i, turned=True)
                        if i:
                            put("sc", b, i - 1)
                    put("new", b, turned=True)
                    put("sc", b, 4)
                put("soft", gi)
            if gi:
                for i in range(3):
                    put("pt", gi - 1, i, turned=True)
                put("pv", 2 * (gi - 1))
                put("pv", 2 * (gi - 1) + 1)
                put("oe", gi - 1)
                if gi % 2 == 0:
                    put("ot", gi // 2 - 1, turned=True)
            if gi < 4:
                put("rc", gi)

        def bank_of(ev):
            return 4 + tiles_of[ev] % 2

        def out_of_bank(n):
            return (s_tgv, n // 2 + 1) if n % 2 == 0 else (s_tga, n // 2 + 1)

        def rows_of(b):
            return slice(32 * (b % 4), 32 * (b % 4) + 32)

        def grp_rows(gi):
            return slice(64 * (gi % 2), 64 * (gi % 2) + 64)

        def sp_sample(sp):
            for a in range(2):
                sp.dma_start(GR[:, a, :], gate_dram[4 * a:4 * a + 4].rearrange("b g t c -> (b g t) c")).then_inc(s_gr, 16)
            sp.wait_ge(s_al, 4)
            sp.dma_start(KCA[:, :, :], ab_dram[:, :, 0, :].rearrange("b n c -> n b c")).then_inc(s_kab, 16)
            for a in range(2):
                for n0, n1 in ((0, 112), (112, NCS)):
                    sp.dma_start(KCB[a][n0:n1, :, :], ab_dram[4 * a:4 * a + 4, n0 + 1:n1 + 1, 1, :]
                                 .rearrange("b n c -> n b c")).then_inc(s_kab, 16)
            sp.wait_ge(s_done_attn, 1)
            sp.dma_start(VN[:, 0, :, :], o_kvs_s[0, :, :, 1].rearrange("b t g d -> t b (g d)")).then_inc(s_vn, 16)
            sp.dma_start(VN[:, 1, :, :], o_win_s[0, :, WIN - DS:WIN, 1].rearrange("b t g d -> t b (g d)")).then_inc(s_vn, 16)
            for b in range(DB):
                if b >= 4:
                    sp.wait_ge(s_pvb, b - 3)
                sp.dma_start(WCA[:, b % 4, :, :], state_win_kv[0, b].rearrange("(p k) x g d -> p k (x g d)", p=P))\
                    .then_inc(s_wc[b % 4], 16)

        def pool_sample(po, link):
            def gather(b):
                if b >= 4:
                    po.wait_ge(s_pvb, b - 3)
                po.indirect_dma_start(out=RING[:, b % 4, :], out_offset=None, in_=sel_chunks,
                                      in_offset=bass.IndirectOffsetOnAxis(ap=idx[:, 24 + b:25 + b], axis=0))\
                    .then_inc(s_ring[b % 4], 16)

            po.wait_ge(s_done_attn, 1)
            for b in range(4):
                gather(b)
            link(po.memset(LT[:, :, :], 1.0))
            po.affine_select(out=LT[:, :, :], in_=LT[:, :, :], compare_op=ALU.is_ge, fill=0.0, base=-1,
                             pattern=[[1, NFREE], [-1, NFREE]], channel_multiplier=0).then_inc(s_lt, 1)
            link(po.memset(GSM[:, :], 0.0))
            for g in range(GROUP):
                link(po.affine_select(out=GSM[:, :].rearrange("p (a g t) -> p a g t", g=GROUP, t=DS),
                                      in_=GSM[:, :].rearrange("p (a g t) -> p a g t", g=GROUP, t=DS),
                                      compare_op=ALU.not_equal, fill=1.0, base=-DS * g,
                                      pattern=[[-16, 8], [0, GROUP], [-1, DS]], channel_multiplier=1))
            po.sem_inc(s_gsm2, 1)
            for gi in range(4):
                for b in (2 * gi + 4, 2 * gi + 5):
                    if b < DB:
                        gather(b)

        def pe_sample(pe):
            pe.wait_ge(s_done_attn, 1)
            pe.wait_ge(s_kc, 2)
            for b in range(DB):
                ins = pe.transpose(PS[:, b // 4, (b % 4) * P:(b % 4) * P + NCS], KCA[0:NCS, b, 0:P], ident[0:NCS, 0:NCS])
            ins.then_inc(s_kct2, 1)
            pe.wait_ge(s_kct2e, 1)
            for b in range(DB):
                ins = pe.matmul(PS[rows_of(b), 2 + b // 4, 0:NCS], QBD[:, b, :], KCTS[:, b, 0:NCS], start=True, stop=True)
            ins.then_inc(s_csc, 1)
            pe.wait_ge(s_gsm2, 1)
            for a in range(2):
                pe.wait_ge(s_pcn, a + 1)
                pe.matmul(PS[:, 4 + a, 0:P], GSM[:, :], PC[:, a, :], start=True, stop=True).then_inc(s_gs, 1)
            pe.wait_ge(s_pcg, 2)
            for a in range(2):
                ins = pe.transpose(PS[:, 6, a * P:a * P + P], PC[:, a, :], ident[:, :])
            ins.then_inc(s_pct, 1)
            pe.wait_ge(s_ptc, 1)
            for ev in EV:
                if ev in tiles_of and tiles_of[ev] >= 2:
                    pe.wait_ge(*out_of_bank(tiles_of[ev] - 2))
                if ev[0] == "kt":
                    _, b, i = ev
                    if i == 0:
                        pe.wait_ge(s_ring[b % 4], 16 * (b // 4 + 1))
                        pe.wait_ge(s_wc[b % 4], 16 * (b // 4 + 1))
                    for c in range(4):
                        k = RING[:, b % 4, (4 * i + c) * 256:(4 * i + c) * 256 + P] if i < 4 else WCA[:, b % 4, c, 0:P]
                        ins = pe.transpose(PS[:, bank_of(ev), c * P:c * P + P], k, ident[:, :])
                    ins.then_inc(s_tg, 1)
                elif ev[0] == "sc":
                    _, b, i = ev
                    pe.wait_ge(*out_of_bank(tiles_of[("kt", b, i)]))
                    if i == 0 and b >= 4 and b % 2 == 0:
                        pe.wait_ge(s_ss, b // 2 - 1)
                    bank, k = (i, KTS[:, i * 512:i * 512 + 512]) if i < 4 else (6, KTW[:, :])
                    pe.matmul(PS[rows_of(b), bank, :], QBD[:, b, :], k, start=True, stop=True).then_inc(s_ksc, 1)
                elif ev[0] == "new":
                    b = ev[1]
                    pe.matmul(PS[rows_of(b), bank_of(ev), 0:DS], QBD[:, b, :], KN[:, 0, DS * b:DS * b + DS], start=True, stop=True)
                    pe.matmul(PS[rows_of(b), bank_of(ev), DS:2 * DS], QBD[:, b, :], KN[:, 1, DS * b:DS * b + DS],
                              start=True, stop=True).then_inc(s_tg, 1)
                elif ev[0] == "pt":
                    _, gi, i = ev
                    r = grp_rows(gi)
                    bank = bank_of(ev)
                    pe.wait_ge(s_esc, 2 * gi + (2 if i == 2 else 1))
                    if i < 2:
                        for c in range(8):
                            ins = pe.transpose(PS[:, bank, 64 * c:64 * c + 64], SS[r, (8 * i + c) * P:(8 * i + c + 1) * P], ident[r, r])
                    else:
                        for c in range(4):
                            pe.transpose(PS[:, bank, 64 * c:64 * c + 64], SW[r, c * P:c * P + P], ident[r, r])
                        pe.transpose(PS[0:DS, bank, 256:320], SS[r, PAST:PAST + DS], ident[r, r])
                        ins = pe.transpose(PS[0:DS, bank, 320:384], SW[r, WIN:WIN + DS], ident[r, r])
                    ins.then_inc(s_tg, 1)
                elif ev[0] == "pv":
                    b = ev[1]
                    gi, a, c0 = b // 2, b // 4, 32 * (b % 2)
                    if b == 0:
                        pe.wait_ge(s_vn, 32)
                    if b % 2 == 0:
                        for i in range(3):
                            pe.wait_ge(*out_of_bank(tiles_of[("pt", gi, i)]))
                        if gi >= 2:
                            pe.wait_ge(s_os, gi - 1)
                    terms = [(PTS[:, j, c0:c0 + 32], RING[:, b % 4, j * 256 + P:j * 256 + 256]) for j in range(16)]
                    terms.append((PTN[:, 0, c0:c0 + 32], VN[:, 0, b, :]))
                    terms += [(PTW[:, j, c0:c0 + 32], WCA[:, b % 4, j, P:256]) for j in range(4)]
                    terms.append((PTN[:, 1, c0:c0 + 32], VN[:, 1, b, :]))
                    terms.append((PTC[0:NCS, a, rows_of(b)], KCA[0:NCS, b, P:256]))
                    for n, (p, w) in enumerate(terms):
                        ins = pe.matmul(PS[rows_of(b), 7, 0:P], p, w, start=(n == 0), stop=(n == len(terms) - 1))
                    ins.then_inc(s_pvb, 1)
                elif ev[0] == "ot":
                    pe.wait_ge(s_os, 2 * ev[1] + 2)
                    pe.transpose(PS[:, bank_of(ev), 0:P], OS[:, ev[1], :], ident[:, :]).then_inc(s_tg, 1)

        def take_tile(eng, copy, ev, sem):
            n = tiles_of[ev]
            eng.wait_ge(s_tg, n + 1)
            bank = bank_of(ev)
            if ev[0] == "kt":
                _, b, i = ev
                if b:
                    eng.wait_ge(s_ksc, 5 * (b - 1) + i + 1)
                ins = copy(KTS[:, i * 512:i * 512 + 512] if i < 4 else KTW[:, :], PS[:, bank, :])
            elif ev[0] == "new":
                r = rows_of(ev[1])
                ins = copy(SNEW[r, :], PS[r, bank, 0:2 * DS])
            elif ev[0] == "pt":
                _, gi, i = ev
                if gi:
                    eng.wait_ge(s_pvb, 2 * gi)
                if i < 2:
                    ins = copy(PTS[:, 8 * i:8 * i + 8, :], PS[:, bank, :].rearrange("p (j r) -> p j r", j=8))
                else:
                    copy(PTW[:, :, :], PS[:, bank, 0:256].rearrange("p (j r) -> p j r", j=4))
                    ins = copy(PTN[:, :, :], PS[0:DS, bank, 256:384].rearrange("p (j r) -> p j r", j=2))
            return ins.then_inc(sem, 1)

        def act_sample(act):
            copy = lambda o, i: act.activation(o, i, ACT.Copy)
            act.wait_ge(s_kct2, 1)
            copy(KCTS[:, :, 0:NCS], PS[:, 0:2, :].rearrange("p a (b n) -> p (a b) n", b=4)[:, :, 0:NCS]).then_inc(s_kct2e, 1)
            for a in range(2):
                act.wait_ge(s_cnm, a + 1)
                act.activation(PC[:, a, 0:NCS], PS[:, 2 + a, 0:NCS], ACT.Exp, bias=ENM[:, a:a + 1], scale=SCALE,
                               accum_out=EDN[:, a:a + 1]).then_inc(s_cex, 1)
            act.wait_ge(s_pct, 1)
            copy(PTC[:, :, :], PS[:, 6, 0:2 * P].rearrange("p (a r) -> p a r", a=2)).then_inc(s_ptc, 1)
            for ev in EV:
                if ev in tiles_of and tiles_of[ev] % 2:
                    if ev[0] == "ot":
                        continue
                    take_tile(act, copy, ev, s_tga)
                elif ev[0] == "soft":
                    gi = ev[1]
                    r = grp_rows(gi)
                    for i, x in enumerate((SS, SW)):
                        act.wait_ge(s_enm, 2 * gi + i + 1)
                        act.activation(x[r, :], x[r, :], ACT.Exp, bias=ENM[r, 2 + i:3 + i], scale=SCALE,
                                       accum_out=EDN[r, 2 + i:3 + i]).then_inc(s_eex, 1)
            for a in range(2):
                act.wait_ge(s_o2, a + 1)
                act.activation(XH[:, 4:8, SEQ + 16 * a:SEQ + 16 * a + 16], O2[:, a, :].rearrange("p (g t) -> p g t", g=4),
                               ACT.Copy).then_inc(s_o2h, 1)

        def dve_sample_early(v, link):
            v.wait_ge(s_tmt, NTT)
            link(v.memset(QBD[:, :, :], 0.0))
            for h in range(2):
                hb = HD * h
                v.tensor_copy(QBD[hb:hb + HD, :, 16 * h:16 * h + 16].rearrange("p b (g t) -> p b g t", g=GROUP),
                              Q[hb:hb + HD, :, SEQ:T].rearrange("p g (b t) -> p b g t", t=DS))
            v.tensor_copy(BGS[:, :, :], BG[:, :, SEQ:T])
            v.tensor_copy(KN[:, 0, :], KV[:, 2, SEQ:T])
            v.tensor_copy(KN[:, 1, :], KV[:, 4, SEQ:T])
            v.wait_ge(s_iota, 1)
            link(v.tensor_scalar(TI[:, 5:6], TI[:, 4:5], 3, None, ALU.bitwise_and))
            v.tensor_copy(TCOL, TI[:, 5:6])
            link(v.tensor_copy(C4, TI[:, 0:4]))
            v.tensor_scalar(NM4, C4, TCOL, NEG, ALU.is_gt, ALU.mult)
            v.tensor_scalar(WM4, C4, TCOL, NEG, ALU.is_le, ALU.mult).then_inc(s_qbd, 1)
            v.wait_ge(s_qbd, 1)

        (s_iota,) = sems("s_iota")

        def pool_sample_early(po):
            po.wait_ge(s_tm, NTT)
            po.iota(TI[:, 0:4], pattern=[[1, 4]], base=0, channel_multiplier=0)
            po.iota(TI[:, 4:5], pattern=[[0, 1]], base=0, channel_multiplier=1).then_inc(s_iota, 1)

        def dve_sample_halves(v):
            v.wait_ge(s_kab, 16 * 5)
            for a in range(2):
                k = KCA[0:NCS, 4 * a:4 * a + 4, :]
                v.tensor_tensor(k, k, KCB[a][0:NCS, :, :], ALU.add).then_inc(s_kc, 1)

        def dve_sample(v, link):
            v.memset(PC[:, :, NCS:P], 0.0)
            v.wait_ge(s_csc, 1)
            for a in range(2):
                link(v.tensor_reduce(EMX[:, a:a + 1], PS[:, 2 + a, 0:NCS], AX, ALU.max))
                v.tensor_scalar(ENM[:, a:a + 1], EMX[:, a:a + 1], -SCALE, None, ALU.mult).then_inc(s_cnm, 1)
            for a in range(2):
                v.wait_ge(s_cex, a + 1)
                link(v.reciprocal(ERC[:, a:a + 1], EDN[:, a:a + 1]))
                v.tensor_scalar(PC[:, a, 0:NCS], PC[:, a, 0:NCS], ERC[:, a:a + 1], None, ALU.mult).then_inc(s_pcn, 1)
            v.wait_ge(s_gr, 32)
            v.wait_ge(s_lt, 1)
            link(v.memset(M32[:, :, :], 0.0))
            for a in range(2):
                v.wait_ge(s_gs, a + 1)
                link(v.tensor_reduce(SCR[:, a, :], PS[:, 4 + a, 0:P].rearrange("p (k e) -> p k e", e=4)[:, :, 0:3], AX, ALU.add))
                v.tensor_scalar(PC[:, a, :], PC[:, a, :], GR[:, a, 0:1], None, ALU.mult).then_inc(s_pcg, 1)
                me = SCR[:, a, 1:1 + NFREE].unsqueeze(2).to_broadcast([P, NFREE, NFREE])
                other = SCR[:, a, 1:1 + NFREE].unsqueeze(1).to_broadcast([P, NFREE, NFREE])
                link(v.tensor_tensor(RE[:, :, :], other, me, ALU.is_equal))
                link(v.tensor_tensor(RE[:, :, :], RE[:, :, :], LT[:, :, :], ALU.mult))
                link(v.tensor_tensor(RG[:, :, :], other, me, ALU.is_gt))
                link(v.tensor_tensor(RG[:, :, :], RG[:, :, :], RE[:, :, :], ALU.add))
                link(v.tensor_reduce(CNT[:, a, 0:NFREE], RG[:, :, :], AX, ALU.add))
                link(v.tensor_scalar(M32[:, a, 1:1 + NFREE], CNT[:, a, 0:NFREE], NPICK - 0.5, NEG, ALU.is_gt, ALU.mult))
                link(v.tensor_copy(M128[:, a, :].rearrange("p (k e) -> p k e", e=4),
                                   M32[:, a, :].unsqueeze(2).to_broadcast([P, NBLK, 4])))
            for ev in EV:
                if ev in tiles_of and ev[0] == "ot":
                    a = ev[1]
                    v.wait_ge(s_tg, tiles_of[ev] + 1)
                    for h in range(2):
                        hb = HD * h
                        o = O2[hb:hb + HD, a, :].rearrange("p (g b t) -> p b g t", g=GROUP, t=DS)
                        src = PS[hb:hb + HD, bank_of(ev), 0:P].rearrange("p (b h g t) -> p b h g t", b=4, h=2, g=GROUP)[:, :, h]
                        bg = BGS[hb:hb + HD, :, 16 * a:16 * a + 16].rearrange("p g (b t) -> p b g t", t=DS)
                        ins = v.tensor_tensor(o, src, bg, ALU.mult)
                    ins.then_inc(s_o2, 1)
                    v.wait_ge(s_o2, a + 1)
                    v.sem_inc(out_of_bank(tiles_of[ev])[0], 1)
                elif ev in tiles_of and tiles_of[ev] % 2 == 0:
                    take_tile(v, v.tensor_copy, ev, s_tgv)
                elif ev[0] == "soft":
                    gi = ev[1]
                    r, a = grp_rows(gi), gi // 2
                    v.wait_ge(s_ksc, 10 * (gi + 1))
                    v.wait_ge(*out_of_bank(tiles_of[("new", 2 * gi)]))
                    v.wait_ge(*out_of_bank(tiles_of[("new", 2 * gi + 1)]))
                    if gi >= 2:
                        v.wait_ge(s_tg, tiles_of[("pt", gi - 2, 2)] + 1)
                    v.tensor_tensor(SS[r, 0:PAST].rearrange("p (j n) -> p j n", j=16),
                                    flat(PS[r, 0:4, :]).rearrange("p (j n) -> p j n", j=16),
                                    M128[r, a, :].unsqueeze(1).to_broadcast([64, 16, P]), ALU.add)
                    v.tensor_tensor(SS[r, PAST:], SNEW[r, 0:DS], NM4[r, :], ALU.add)
                    v.tensor_copy(SW[r, 0:WIN], PS[r, 6, :]).then_inc(s_ss, 1)
                    link(v.tensor_tensor(SW[r, WIN:], SNEW[r, DS:2 * DS], NM4[r, :], ALU.add))
                    first = SW[r, 0:WIN].rearrange("p (k n) -> p k n", k=4)[:, :, 0]
                    link(v.tensor_tensor(first, first, WM4[r, :], ALU.add))
                    for i, x in enumerate((SS, SW)):
                        link(v.tensor_reduce(EMX[r, 2 + i:3 + i], x[r, :], AX, ALU.max))
                        v.tensor_scalar(ENM[r, 2 + i:3 + i], EMX[r, 2 + i:3 + i], -SCALE, None, ALU.mult).then_inc(s_enm, 1)
                elif ev[0] == "rc":
                    gi = ev[1]
                    r = grp_rows(gi)
                    v.wait_ge(s_eex, 2 * gi + 2)
                    a = gi // 2
                    link(v.reciprocal(ERC[r, 2:4], EDN[r, 2:4]))
                    v.tensor_scalar(SS[r, :], SS[r, :], ERC[r, 2:3], GR[r, a, 1:2], ALU.mult, ALU.mult).then_inc(s_esc, 1)
                    v.tensor_scalar(SW[r, :], SW[r, :], ERC[r, 3:4], GR[r, a, 2:3], ALU.mult, ALU.mult).then_inc(s_esc, 1)
                elif ev[0] == "oe":
                    gi = ev[1]
                    r, a = grp_rows(gi), gi // 2
                    v.wait_ge(s_pvb, 2 * gi + 2)
                    v.tensor_copy(OS[r, a, :], PS[r, 7, 0:P]).then_inc(s_os, 1)
            for a in range(2):
                v.wait_ge(s_o2h, a + 1)
                cols = slice(SEQ + 16 * a, SEQ + 16 * a + 16)
                link(v.tensor_tensor(XL[:, 4:8, cols], O2[:, a, :].rearrange("p (g t) -> p g t", g=4), XHf[:, 4:8, cols],
                                     ALU.subtract))

        WOH = at("WOH", [P, KT, D], F32R, 67584)
        WOL = at("WOL", [P, KT, D], F32R, 100352)
        WOR = [at("WOR0", [P, 4, D], F32, 133120), at("WOR1", [P, 4, D], F32, 139520)]
        XR = [at("XR0", [P, 2, D], F32, 149504), at("XR1", [P, 2, D], F32, 155904)]
        R = [at("R0", [P, 3, D], F32, 133120), at("R1", [P, 3, D], F32, 139520)]
        GB = at("GB", [P, 2, D], F32, 189408)
        BST = at("BST", [P, 2, 16], F32, 197600)
        names = ("wor0", "wor1", "wor2", "wor3", "woh", "wol", "gb", "xr0", "xr1", "y", "res", "var", "std", "nrm", "aff", "xt",
                 "xh", "xl", "st0", "st1", "st2", "rq")
        OUT = dict(zip(names, sems(*[f"s_o_{n}" for n in names])))
        LEFT = dict(wor0=48, wor1=48, wor2=48, wor3=48, woh=KT, wol=KT, gb=32, xr0=16 * 5, xr1=16 * 4, y=NTT, res=NTT, var=NTT, std=NTT,
                    nrm=NTT, aff=NTT, xt=0, xh=0, xl=0, st0=48, st1=48, st2=48, rq=NTT)

        def wait_out(eng, layer, name, value):
            eng.wait_ge(OUT[name], value + (LEFT[name] if layer else 0))

        x1_rows = lambda tt: x1_dram[tok(tt), :]
        y_rows = lambda tt: y_prompt[0][tok(tt), :] if tt < NTT - 1 else y_sample.rearrange("b t d -> (b t) d")
        RES_IN = (x_rows, x1_rows)
        RES_OUT = (x1_rows, y_rows)
        W_OUT = (w_out_even[0], w_out_odd[0])

        def sp_out_loads(sp, layer):
            s = OUT
            for tt in range(2):
                sp.dma_start(XR[layer][0:ntok(tt), tt, :], RES_IN[layer](tt)).then_inc(s[f"xr{tt}"], 16)
            for kk in range(KT):
                if kk >= 4:
                    if kk == 4:
                        if layer == 0:
                            sp.wait_ge(s_done_samp, 1)
                        for r, t in enumerate((ln_g, ln_b)):
                            sp.dma_start(GB[:, r, :], t[layer].partition_broadcast(P)).then_inc(s["gb"], 16)
                    wait_out(sp, layer, "wol", kk - 3)
                if layer == 0 and kk >= 4:
                    for h in range(2):
                        r0 = WC + (GROUP * h + kk - 4) * HD
                        sp.dma_start(WOR[layer][HD * h:HD * h + HD, kk % 4, :], W_OUT[0][r0:r0 + HD, :])\
                            .then_inc(s[f"wor{kk % 4}"], 16)
                else:
                    sp.dma_start(WOR[layer][:, kk % 4, :], W_OUT[layer][kk * P:kk * P + P, :]).then_inc(s[f"wor{kk % 4}"], 16)

        def sp_out_tiles(sp, layer):
            s = OUT
            for tt in range(NTT):
                n = ntok(tt)
                if tt + 2 < NTT:
                    wait_out(sp, layer, "res", tt + 1)
                    sp.dma_start(XR[layer][0:ntok(tt + 2), tt % 2, :], RES_IN[layer](tt + 2)).then_inc(s[f"xr{tt % 2}"], 16)
                wait_out(sp, layer, "aff", tt + 1)
                sp.dma_start(RES_OUT[layer](tt), R[layer][0:n, tt % 3, :]).then_inc(s[f"st{tt % 3}"], 16)

        def sp_out_end(sp, layer):
            for i in range(3):
                wait_out(sp, layer, f"st{i}", 16 * (NTT // 3))

        def act_out_weights(act, layer, kks=range(KT)):
            s = OUT
            for kk in kks:
                extra = kk // 4 if layer == 0 else 0
                wait_out(act, layer, f"wor{kk % 4}", 16 * (kk // 4 + 1 + extra))
                act.activation(WOH[:, kk, :], WOR[layer][:, kk % 4, :], ACT.Copy).then_inc(s["woh"], 1)

        def pool_out_weights(po, layer):
            s = OUT
            for kk in range(KT):
                wait_out(po, layer, "woh", kk + 1)
                if layer and kk:
                    po.wait_ge(s_ml, kk)
                po.tensor_tensor(WOL[:, kk, :], WOR[layer][:, kk % 4, :], WOH[:, kk, :].bitcast(F32), ALU.subtract)\
                    .then_inc(s["wol"], 1)

        def pe_out(pe, layer):
            s = OUT

            def turn(tt):
                n = ntok(tt)
                wait_out(pe, layer, "aff", tt + 1)
                if tt >= 2:
                    wait_out(pe, layer, "xl", 2 * (tt - 1))
                for hf in range(2):
                    for j in range(4):
                        ins = pe.transpose(PS[:, 4 + 2 * (tt % 2) + hf, j * P:j * P + n],
                                           R[layer][0:n, tt % 3, (4 * hf + j) * P:(4 * hf + j + 1) * P], ident[0:n, 0:n])
                    ins.then_inc(s["xt"], 1)

            for tt in range(NTT):
                n, b0 = ntok(tt), 2 * (tt % 2)
                if tt >= 2:
                    wait_out(pe, layer, "res", tt - 1)
                for kk in range(KT):
                    if tt == 0:
                        wait_out(pe, layer, "wol", kk + 1)
                    for i, (x, w) in enumerate(((XH, WOH), (XL, WOH), (XH, WOL))):
                        for hf in range(2):
                            ins = pe.matmul(PS[0:n, b0 + hf, :], x[:, kk, tok(tt)], w[:, kk, hf * 512:hf * 512 + 512],
                                            start=(kk == 0 and i == 0), stop=(kk == KT - 1 and i == 2))
                ins.then_inc(s["y"], 1)
                if layer == 0 and tt >= 2:
                    turn(tt - 2)
            if layer == 0:
                turn(NTT - 2)
                turn(NTT - 1)

        def dve_out(v, link, layer):
            s = OUT

            def low(tt):
                n = ntok(tt)
                for hf in range(2):
                    wait_out(v, layer, "xh", 2 * tt + hf + 1)
                    v.tensor_tensor(XL[:, 4 * hf:4 * hf + 4, tok(tt)],
                                    PS[:, 4 + 2 * (tt % 2) + hf, :].rearrange("p (k t) -> p k t", k=4)[:, :, 0:n],
                                    XHf[:, 4 * hf:4 * hf + 4, tok(tt)], ALU.subtract).then_inc(s["xl"], 1)

            for tt in range(NTT):
                n, b0 = ntok(tt), 2 * (tt % 2)
                r, st = R[layer][0:n, tt % 3, :], BST[0:n, tt % 2, :]
                wait_out(v, layer, "y", tt + 1)
                wait_out(v, layer, f"xr{tt % 2}", 16 * (tt // 2 + 1))
                if tt >= 3:
                    wait_out(v, layer, f"st{tt % 3}", 16 * (tt // 3))
                    if layer == 0:
                        wait_out(v, layer, "xt", 2 * (tt - 2))
                ins = v.scalar_tensor_tensor(r, XR[layer][0:n, tt % 2, :], ALPHA, flat(PS[0:n, b0:b0 + 2, :]), ALU.mult, ALU.add)
                ins.then_inc(s["res"], 1)
                wait_out(v, layer, "res", tt + 1)
                v.bn_stats(st[:, 0:6], r[:, 0:512])
                link(v.bn_stats(st[:, 6:12], r[:, 512:1024]))
                link(v.bn_aggr(st[:, 12:14], st[:, 0:12].rearrange("p (a c) -> p a c", a=2)))
                v.tensor_scalar(st[:, 14:15], st[:, 13:14], EPS, None, ALU.add).then_inc(s["var"], 1)
                if layer == 0 and tt >= 3:
                    low(tt - 3)
                wait_out(v, layer, "std", tt + 1)
                link(v.reciprocal(st[:, 15:16], st[:, 14:15]))
                v.tensor_scalar(r, r, st[:, 12:13], st[:, 15:16], ALU.subtract, ALU.mult).then_inc(s["nrm"], 1)
            if layer == 0:
                for tt in range(NTT - 3, NTT):
                    low(tt)

        def act_out(act, layer):
            s = OUT

            def high(tt):
                n = ntok(tt)
                for hf in range(2):
                    wait_out(act, layer, "xt", 2 * tt + hf + 1)
                    act.activation(XH[:, 4 * hf:4 * hf + 4, tok(tt)],
                                   PS[:, 4 + 2 * (tt % 2) + hf, :].rearrange("p (k t) -> p k t", k=4)[:, :, 0:n],
                                   ACT.Copy).then_inc(s["xh"], 1)

            for tt in range(NTT):
                st = BST[0:ntok(tt), tt % 2, 14:15]
                wait_out(act, layer, "var", tt + 1)
                act.activation(st, st, ACT.Sqrt).then_inc(s["std"], 1)
                if layer == 0 and tt >= 2:
                    high(tt - 2)
            if layer == 0:
                high(NTT - 2)
                high(NTT - 1)

        def pool_out(po, layer):
            s = OUT
            wait_out(po, layer, "gb", 32)
            for tt in range(NTT):
                r = R[layer][0:ntok(tt), tt % 3, :]
                wait_out(po, layer, "nrm", tt + 1)
                po.tensor_tensor(r, r, GB[0:ntok(tt), 0, :], ALU.mult).then_inc(s["rq"], 1)
                wait_out(po, layer, "rq", tt + 1)
                po.tensor_tensor(r, r, GB[0:ntok(tt), 1, :], ALU.add).then_inc(s["aff"], 1)

        V = at("V", [P, KT, VW + DB * VS], F32, 67584)
        GT = at("GT", [P, KT, T], F32, 105696)
        SA = at("SA", [P, VW + DB * VS], F32, 139488)
        SB = at("SB", [P, VW + DB * VS], F32, 144256)
        GRAW = at("GRAW", [P, 8, 256], F32, 149056)
        VLAST = at("VLAST", [P, KT, 47], F32, 157248)
        STP = at("STP", [120, D], F32, 197728)
        VROW = at("VROW", [NSAMP, 2, D], F32, 197728)
        GH = at("GH", [P, 8, 256], F32R, 173024)
        GL = at("GL", [P, 8, 256], F32R, 181216)
        RT = at("RT", [P, 16], F32, 158784)
        RTI = at("RTI", [P, 16], F32, 158848)
        (s_stp, s_stt, s_sti, s_wh2, s_wl2, s_mm2, s_ev2, s_vl, s_d, s_dh, s_dl, s_graw, s_gh, s_gl, s_gm, s_ge, s_mh,
         s_ml, s_vt, s_ve, s_rt) = sems(
            "s_stp", "s_stt", "s_sti", "s_wh2", "s_wl2", "s_mm2", "s_ev2", "s_vl", "s_d", "s_dh", "s_dl", "s_graw",
            "s_gh", "s_gl", "s_gm", "s_ge", "s_mh", "s_ml", "s_vt", "s_ve", "s_rt")
        s_raw2 = sems("s_raw2_0", "s_raw2_1")
        NM2 = 2 * KT
        w_in2 = w_in_odd[0].rearrange("(k p) e -> p k e", p=P)

        def load_w2(sp, m):
            sp.dma_start(WRAW[:, m % 2, :, :], w_in2[:, :, m * P:m * P + P]).then_inc(s_raw2[m % 2], 16)

        def sp_mixer(sp):
            sp.dma_start(STP[:, :], state_pool[0].rearrange("b t c -> (b t) c")).then_inc(s_stp, 16)
            load_w2(sp, 0)
            load_w2(sp, 1)
            sp_out_tiles(sp, 0)
            for m in range(2, NM2):
                sp.wait_ge(s_wl2, m - 1)
                load_w2(sp, m)
                if m == 4:
                    sp.wait_ge(s_ve2, 1)
                    sp.dma_start(GRAW[:, :, :], w_pool_grp[0].rearrange("g (k p) e -> p (g k) e", k=2)).then_inc(s_graw, 16)
            sp.wait_ge(s_ve, 2)
            sp.dma_start(o_pool_p[0, 0], VROW[0:PMAX - 1, 0, :]).then_inc(s_out, 16)
            outs[0] += 16
            for b in range(DB):
                sp.dma_start(o_pool_s[0, b, PMAX - 1 - DS:PMAX - 1], VROW[DS * b:DS * b + DS, 1, :]).then_inc(s_out, 16)
                outs[0] += 16

        (s_ve2,) = sems("s_ve2")

        def pe_mixer(pe):
            pe.wait_ge(s_stp, 16)
            wait_out(pe, 0, "xl", 2 * NTT)
            for hf in range(2):
                for j in range(4):
                    ins = pe.transpose(PS[:, 6 + hf, 120 * j:120 * j + 120], STP[:, (4 * hf + j) * P:(4 * hf + j + 1) * P],
                                       ident[0:120, 0:120])
            ins.then_inc(s_stt, 1)
            pe.wait_ge(s_ev2, 1)
            with pe.Fori(0, NM2 // 2) as pair:
                for slot in range(2):
                    pe.wait_ge(s_wl2, pair * 2 + (slot + 1))
                    pe.wait_ge(s_ev2, pair * 2 + (slot + 1))
                    b0 = 3 * slot
                    for kk in range(KT):
                        for n, (w, x) in enumerate(((WH, XH), (WH, XL), (WL, XH))):
                            for c in range(3):
                                ins = pe.matmul(PS[:, b0 + c, 0:CH], w[:, slot, kk, :], x[:, kk, c * CH:(c + 1) * CH],
                                                start=(kk == 0 and n == 0), stop=(kk == KT - 1 and n == 2))
                    ins.then_inc(s_mm2, 1)
            pe.wait_ge(s_vl, KT)
            pe.wait_ge(s_sti, 1)
            for part, (a, b) in enumerate(((0, 15), (15, 47))):
                if part:
                    pe.wait_ge(s_ve, 1)
                for ct in range(KT):
                    ins = pe.transpose(PS[0:b - a, 6 + ct // 4, (ct % 4) * P:(ct % 4) * P + P], VLAST[:, ct, a:b], ident[:, :])
                ins.then_inc(s_vt, 1)
            pe.wait_ge(s_gl, 1)
            pe.wait_ge(s_ev2, NM2 + 2)
            for g in range(4):
                for e in range(2):
                    if g:
                        pe.wait_ge(s_ge, 2 * (g - 1) + e + 1)
                    for kk in range(2):
                        if e == 0:
                            pe.wait_ge(s_dl, 2 * g + kk + 1)
                        for n, (w, x) in enumerate(((GH, XH), (GH, XL), (GL, XH))):
                            for c in range(3):
                                ins = pe.matmul(PS[:, 3 * e + c, 0:CH], w[:, 2 * g + kk, e * P:e * P + P],
                                                x[:, 2 * g + kk, c * CH:(c + 1) * CH],
                                                start=(kk == 0 and n == 0), stop=(kk == 1 and n == 2))
                    ins.then_inc(s_gm, 1)

        def act_mixer(act):
            def high(m):
                act.wait_ge(s_raw2[m % 2], 16 * (m // 2 + 1))
                if m >= 2:
                    act.wait_ge(s_mm2, m - 1)
                act.activation(WH[:, m % 2, :, :], WRAW[:, m % 2, :, :], ACT.Copy).then_inc(s_wh2, 1)

            high(0)
            high(1)
            act_out(act, 0)
            for m in range(NM2):
                b0 = 3 * (m % 2)
                act.wait_ge(s_mm2, m + 1)
                if m < KT:
                    act.activation(V[:, m, PMAX - 1:PMAX - 1 + 2 * CH].rearrange("p (a c) -> p a c", a=2),
                                   PS[:, b0:b0 + 2, 0:CH], ACT.Copy)
                    act.activation(V[:, m, PMAX - 1 + 2 * CH:VW], PS[:, b0 + 2, 0:SEQ - 2 * CH], ACT.Copy)
                    act.activation(samples(V[:, m, VW:])[:, :, PMAX - 1:VS],
                                   PS[:, b0 + 2, SEQ - 2 * CH:CH].rearrange("p (b t) -> p b t", b=DB),
                                   ACT.Copy).then_inc(s_ev2, 1)
                else:
                    act.activation(GT[:, m - KT, :].rearrange("p (a c) -> p a c", a=3), PS[:, b0:b0 + 3, 0:CH],
                                   ACT.Silu).then_inc(s_ev2, 1)
                if m + 2 < NM2:
                    high(m + 2)
            act.wait_ge(s_graw, 16)
            act.activation(GH[:, :, :], GRAW[:, :, :], ACT.Copy).then_inc(s_gh, 1)
            for ct in range(KT):
                act.wait_ge(s_d, ct + 1)
                act.activation(XH[:, ct, 0:SEQ], V[:, ct, PMAX - 1:VW], ACT.Copy)
                act.activation(XH[:, ct, SEQ:T].rearrange("p (b t) -> p b t", b=DB),
                               samples(V[:, ct, VW:])[:, :, PMAX - 1:VS], ACT.Copy).then_inc(s_dh, 1)
            for ct in range(KT):
                act.wait_ge(s_gm, 2 * (ct // 2) + 2)
                act.wait_ge(s_ge, ct + 1)
                act.activation(XH[:, ct, :], GT[:, ct, :], ACT.Copy).then_inc(s_mh, 1)
                if ct % 2:
                    act.wait_ge(s_dl, KT)
                    act_out_weights(act, 1, (ct - 1, ct))

        def pool_mixer_weights(po):
            for m in range(2):
                po.wait_ge(s_wh2, m + 1)
                po.tensor_tensor(WL[:, m, :, :], WRAW[:, m, :, :], WH[:, m, :, :].bitcast(F32), ALU.subtract).then_inc(s_wl2, 1)
            pool_out(po, 0)
            for m in range(2, NM2):
                po.wait_ge(s_wh2, m + 1)
                po.tensor_tensor(WL[:, m % 2, :, :], WRAW[:, m % 2, :, :], WH[:, m % 2, :, :].bitcast(F32),
                                 ALU.subtract).then_inc(s_wl2, 1)
            po.wait_ge(s_gh, 1)
            po.tensor_tensor(GL[:, :, :], GRAW[:, :, :], GH[:, :, :].bitcast(F32), ALU.subtract).then_inc(s_gl, 1)

        def dve_mixer(v, link):
            for i in range(3):
                wait_out(v, 0, f"st{i}", 16 * (NTT // 3))
            v.sem_inc(s_ve2, 1)
            v.wait_ge(s_stt, 1)
            v.memset(V[:, :, 0:PMAX - 1], 0.0)
            for t in range(16):
                ins = v.memset(RT[:, t:t + 1], 1.0 + t)
            link(ins)
            link(v.reciprocal(RT[:, :], RT[:, :]))
            for ct in range(KT):
                ins = v.tensor_copy(samples(V[:, ct, VW:])[:, :, 0:PMAX - 1],
                                    PS[:, 6 + ct // 4, 120 * (ct % 4):120 * (ct % 4) + 120].rearrange("p (b t) -> p b t", b=DB))
            link(ins)
            v.sem_inc(s_sti, 1)
            v.sem_inc(s_ev2, 2)
            n = VW + DB * VS
            for ct in range(KT):
                w = 2 << (ct // 2)
                v.wait_ge(s_ev2, 2 + ct + 1)
                x = V[:, ct, :]
                v.tensor_copy(VLAST[:, ct, 0:15], V[:, ct, SEQ:VW])
                v.tensor_copy(VLAST[:, ct, 15:47].rearrange("p (b t) -> p b t", b=DB),
                              samples(V[:, ct, VW:])[:, :, PMAX - 1:VS]).then_inc(s_vl, 1)
                link(v.tensor_tensor(SA[:, 1:n], x[:, 1:n], x[:, 0:n - 1], ALU.add))
                cur_, oth, sh = SA, SB, 2
                while sh < w:
                    lo = 2 * sh - 1
                    link(v.tensor_tensor(oth[:, lo:n], cur_[:, lo:n], cur_[:, lo - sh:n - sh], ALU.add))
                    cur_, oth, sh = oth, cur_, 2 * sh
                e = cur_[:, PMAX - 1:PMAX - 1 + w - 1]
                link(v.scalar_tensor_tensor(e, e, float(w), RT[:, 0:w - 1], ALU.mult, ALU.mult))
                pr, ps = V[:, ct, PMAX - 1:VW], samples(V[:, ct, VW:])[:, :, PMAX - 1:VS]
                link(v.scalar_tensor_tensor(pr, cur_[:, PMAX - 1:VW], 1.0 / w, pr, ALU.mult, ALU.subtract))
                link(v.scalar_tensor_tensor(ps, samples(cur_[:, VW:])[:, :, PMAX - 1:VS], 1.0 / w, ps, ALU.mult,
                                            ALU.subtract))
            v.wait_ge(s_vt, 1)
            v.tensor_copy(VROW[0:15, 0, :], flat(PS[0:15, 6:8, :])).then_inc(s_ve, 1)
            v.wait_ge(s_vt, 2)
            v.tensor_copy(VROW[:, 1, :], flat(PS[0:NSAMP, 6:8, :])).then_inc(s_ve, 1)
            v.wait_ge(s_mm2, NM2)
            v.sem_inc(s_d, KT)
            for ct in range(KT):
                v.wait_ge(s_dh, ct + 1)
                v.tensor_tensor(XL[:, ct, 0:SEQ], V[:, ct, PMAX - 1:VW], XHf[:, ct, 0:SEQ], ALU.subtract)
                v.tensor_tensor(XL[:, ct, SEQ:T].rearrange("p (b t) -> p b t", b=DB),
                                samples(V[:, ct, VW:])[:, :, PMAX - 1:VS],
                                XHf[:, ct, SEQ:T].rearrange("p (b t) -> p b t", b=DB), ALU.subtract).then_inc(s_dl, 1)
            for g in range(4):
                for e in range(2):
                    ct = 2 * g + e
                    v.wait_ge(s_gm, ct + 1)
                    gt = GT[:, ct, :].rearrange("p (a c) -> p a c", a=3)
                    v.scalar_tensor_tensor(gt, PS[:, 3 * e:3 * e + 3, 0:CH], PSC[:, ct:ct + 1], gt, ALU.mult,
                                           ALU.mult).then_inc(s_ge, 1)
                for e in range(2):
                    ct = 2 * g + e
                    v.wait_ge(s_mh, ct + 1)
                    v.tensor_tensor(XL[:, ct, :], GT[:, ct, :], XHf[:, ct, :], ALU.subtract).then_inc(s_ml, 1)


        def sp_late(sp):
            sp_sample(sp)
            sp.wait_ge(s_pvb, 6)
            sp_out_loads(sp, 0)
            sp_mixer(sp)
            sp_out_end(sp, 0)
            sp.wait_ge(s_d, KT)
            sp.wait_ge(s_gl, 1)
            sp_out_loads(sp, 1)
            sp_out_tiles(sp, 1)
            sp_out_end(sp, 1)

        s_done_attn, s_done_samp = sems("s_done_attn", "s_done_samp")

        def pool_late(po, link):
            pool_sample_early(po)
            pool_attention(po)
            pool_sample(po, link)
            pool_out_weights(po, 0)
            pool_mixer_weights(po)
            pool_out_weights(po, 1)
            pool_out(po, 1)

        def act_late(act):
            act_attention(act)
            act_sample(act)
            act.wait_ge(s_done_samp, 1)
            act_out_weights(act, 0)
            act_mixer(act)
            act_out(act, 1)

        def dve_late(v, link):
            dve_sample_early(v, link)
            dve_attention(v, link)
            v.wait_ge(s_ol, 16)
            v.wait_ge(s_stored, 1)
            v.sem_inc(s_done_attn, 1)
            dve_sample(v, link)
            v.sem_inc(s_done_samp, 1)
            dve_out(v, link, 0)
            dve_mixer(v, link)
            dve_out(v, link, 1)

        def pe_late(pe):
            pe_attention(pe)
            pe_sample(pe)
            pe.wait_ge(s_done_samp, 1)
            pe_out(pe, 0)
            pe_mixer(pe)
            pe.wait_ge(s_ml, KT)
            pe_out(pe, 1)

        block = ctx.enter_context(nc.Block())

        @block.sync
        def _(sp):
            sp_program(sp)

        @block.gpsimd
        def _(po):
            pool_program(po)

        @block.scalar
        def _(act):
            act_program(act)

        @block.vector
        def _(v):
            dve_program(v)

        @block.tensor
        def _(pe):
            pe_program(pe)


_INS = ['x_prompt', 'x_sample', 'cache_kv_cmp', 'cache_kv_sel', 'state_win_kv', 'state_conv', 'state_pool', 'page_table',
        'w_in_even', 'w_cmp', 'conv_w', 'conv_b', 'conv_ln_g', 'conv_ln_b', 'w_out_even', 'w_in_odd', 'w_pool_grp',
        'pool_scale', 'w_out_odd', 'ln_g', 'ln_b']
_OUTS = [(1, SEQ, D), (DB, DS, D),
         (1, 1, SEQ, 2, 2, HD), (1, 1, SEQ, 2, 2, HD), (1, 1, WIN, 2, 2, HD), (1, 1, CW - 1, WC), (1, 1, PMAX - 1, D),
         (1, DB, DS, 2, 2, HD), (1, DB, DS, 2, 2, HD), (1, DB, WIN, 2, 2, HD), (1, DB, CW - 1, WC), (1, DB, PMAX - 1, D)]


def kernel(**inputs):
    import concourse.bacc as bacc
    from concourse.bass_utils import run_bass_kernel_spmd

    nc = bacc.Bacc("TRN2", target_bir_lowering=False, num_devices=1)
    arrays, args = {}, []
    for name in _INS:
        a = np.ascontiguousarray(inputs[name])
        arrays["in_" + name] = a
        args.append(nc.dram_tensor("in_" + name, a.shape, mybir.dt.from_np(a.dtype), kind="ExternalInput").ap())
    for i, shape in enumerate(_OUTS):
        args.append(nc.dram_tensor(f"out_{i}", shape, F32, kind="ExternalOutput").ap())
    program(nc, *args)
    r = run_bass_kernel_spmd(nc, [arrays], core_ids=[0])
    return tuple(r.results[0][f"out_{i}"] for i in range(len(_OUTS)))
```
